# Optimizing a Trainium2 kernel written in Bass

```python
import math
import jax, jax.numpy as jnp
from jax import lax
import numpy as np

D_MODEL = 1024
BATCH = 1
SEQ = 256
DEPTH = 1

ATTN_WIDTH = D_MODEL // 2
N_ATTN_HEADS = 8
HEAD_DIM = ATTN_WIDTH // N_ATTN_HEADS
LRU_WIDTH = D_MODEL - ATTN_WIDTH
N_LRU_BLOCKS = 8
LRU_BLOCK = LRU_WIDTH // N_LRU_BLOCKS
CONV_WIDTH = 4
LRU_C = 8.0
MOBA_BLOCK = 256
MOBA_TOPK = 3
Q_CHUNK = 16
D_FF = 4 * D_MODEL
IN_WIDTH = 3 * ATTN_WIDTH + 2 * LRU_WIDTH
LN_EPS = 1e-5
DEEPNORM_ALPHA = (2.0 * DEPTH) ** 0.25
DEEPNORM_BETA = (8.0 * DEPTH) ** -0.25
NEG_INF = -1e30

kernel_name = "hymba_moba_rglru_deepnorm_layer"

def layer_norm(x, g, b):
    xf = x.astype(jnp.float32)
    mu = jnp.mean(xf, axis=-1, keepdims=True)
    var = jnp.mean(jnp.square(xf - mu), axis=-1, keepdims=True)
    y = (xf - mu) * lax.rsqrt(var + LN_EPS) * g.astype(jnp.float32) + b.astype(jnp.float32)
    return y.astype(x.dtype)

def alibi_slopes(n_heads):
    h = jnp.arange(1, n_heads + 1, dtype=jnp.float32)
    return jnp.exp2(-8.0 * h / n_heads)

def moba_attention(q, k, v):
    B, S, H, Dh = q.shape
    nb = -(-S // MOBA_BLOCK)
    sp = nb * MOBA_BLOCK
    pad = sp - S

    def prep(t):
        t = jnp.pad(t, ((0, 0), (0, pad), (0, 0), (0, 0)))
        return t.transpose(0, 2, 1, 3)

    q, k, v = prep(q), prep(k), prep(v)
    kb = k.reshape(B, H, nb, MOBA_BLOCK, Dh)
    vb = v.reshape(B, H, nb, MOBA_BLOCK, Dh)
    n_chunks = sp // Q_CHUNK
    topk = min(MOBA_TOPK, nb - 1)
    q_blk = jnp.arange(sp) // MOBA_BLOCK

    if topk > 0:
        k_mean = jnp.mean(kb.astype(jnp.float32), axis=3)
        gate = jnp.einsum('bhtd,bhnd->bhtn', q.astype(jnp.float32), k_mean)
        fully_past = jnp.arange(nb)[None, :] < q_blk[:, None]
        gate = jnp.where(fully_past, gate, NEG_INF)
        _, sel = lax.top_k(gate, topk)
        sel = sel.astype(jnp.int32)
    else:
        sel = jnp.zeros((B, H, sp, 0), jnp.int32)
    sel_c = sel.reshape(B, H, n_chunks, Q_CHUNK, topk).transpose(2, 0, 1, 3, 4)
    q_c = q.reshape(B, H, n_chunks, Q_CHUNK, Dh).transpose(2, 0, 1, 3, 4)

    slopes = alibi_slopes(H)[None, :, None, None]
    bi = jnp.arange(B)[:, None, None, None]
    hi = jnp.arange(H)[None, :, None, None]
    key_off = jnp.arange(MOBA_BLOCK)
    scale = Dh ** -0.5

    def chunk_fn(args):
        c, qc, selc = args
        t = c * Q_CHUNK + jnp.arange(Q_CHUNK)
        own = (c * Q_CHUNK) // MOBA_BLOCK
        k_own = lax.dynamic_index_in_dim(kb, own, axis=2, keepdims=False)
        v_own = lax.dynamic_index_in_dim(vb, own, axis=2, keepdims=False)
        s_own = own * MOBA_BLOCK + key_off
        lo = jnp.einsum('bhqd,bhcd->bhqc', qc, k_own).astype(jnp.float32) * scale
        lo = lo - slopes * (t[:, None] - s_own[None, :])
        lo = jnp.where(s_own[None, :] <= t[:, None], lo, NEG_INF)
        kg = kb[bi, hi, selc]
        vg = vb[bi, hi, selc]
        s_past = selc[..., None] * MOBA_BLOCK + key_off
        lp = jnp.einsum('bhqd,bhqkcd->bhqkc', qc, kg).astype(jnp.float32) * scale
        lp = lp - slopes[..., None] * (t[:, None, None] - s_past)
        lp = jnp.where((selc < own)[..., None], lp, NEG_INF)
        n_past = topk * MOBA_BLOCK
        lp = lp.reshape(B, H, Q_CHUNK, n_past)
        p = jax.nn.softmax(jnp.concatenate([lp, lo], axis=-1), axis=-1).astype(v.dtype)
        out = jnp.einsum('bhqn,bhqnd->bhqd', p[..., :n_past],
                         vg.reshape(B, H, Q_CHUNK, n_past, Dh))
        out = out + jnp.einsum('bhqc,bhcd->bhqd', p[..., n_past:], v_own)
        return out

    out = lax.map(chunk_fn, (jnp.arange(n_chunks, dtype=jnp.int32), q_c, sel_c))
    out = out.transpose(1, 0, 3, 2, 4).reshape(B, sp, H * Dh)
    return out[:, :S]

def causal_depthwise_conv(x, w, b):
    S = x.shape[1]
    xp = jnp.pad(x, ((0, 0), (CONV_WIDTH - 1, 0), (0, 0)))
    y = b
    for kk in range(CONV_WIDTH):
        y = y + xp[:, kk:kk + S] * w[kk]
    return y

def block_diag_linear(x, w, b):
    xb = x.reshape(x.shape[0], x.shape[1], N_LRU_BLOCKS, LRU_BLOCK)
    y = jnp.einsum('bsnd,nde->bsne', xb, w).reshape(x.shape)
    return y + b

def rg_lru(x, w_rg, b_rg, w_ig, b_ig, lam):
    xf = x.astype(jnp.float32)
    r = jax.nn.sigmoid(block_diag_linear(x, w_rg, b_rg).astype(jnp.float32))
    i = jax.nn.sigmoid(block_diag_linear(x, w_ig, b_ig).astype(jnp.float32))
    log_a = -LRU_C * r * jax.nn.softplus(-lam.astype(jnp.float32))
    a = jnp.exp(log_a)
    u = jnp.sqrt(-jnp.expm1(2.0 * log_a)) * (i * xf)

    def combine(left, right):
        a1, b1 = left
        a2, b2 = right
        return a1 * a2, a2 * b1 + b2

    _, h = lax.associative_scan(combine, (a, u), axis=1)
    return h.astype(x.dtype)

def setup_inputs(seed: int = 0) -> dict:
    key = jax.random.key(seed)
    ks = jax.random.split(key, 20)
    f32 = jnp.float32
    L = DEPTH
    w_in = jax.random.normal(ks[1], (L, D_MODEL, IN_WIDTH), f32) * D_MODEL ** -0.5
    w_in = w_in.at[:, :, 2 * ATTN_WIDTH:3 * ATTN_WIDTH].multiply(DEEPNORM_BETA)
    conv_w = jax.random.normal(ks[2], (L, CONV_WIDTH, LRU_WIDTH), f32) * CONV_WIDTH ** -0.5
    conv_b = 0.02 * jax.random.normal(ks[3], (L, LRU_WIDTH), f32)
    w_rg = jax.random.normal(ks[4], (L, N_LRU_BLOCKS, LRU_BLOCK, LRU_BLOCK), f32) * LRU_BLOCK ** -0.5
    b_rg = 0.02 * jax.random.normal(ks[5], (L, LRU_WIDTH), f32)
    w_ig = jax.random.normal(ks[6], (L, N_LRU_BLOCKS, LRU_BLOCK, LRU_BLOCK), f32) * LRU_BLOCK ** -0.5
    b_ig = 0.02 * jax.random.normal(ks[7], (L, LRU_WIDTH), f32)
    a_c = jax.random.uniform(ks[8], (L, LRU_WIDTH), f32, 0.9, 0.999)
    a0 = a_c ** (1.0 / LRU_C)
    lru_lambda = jnp.log(a0) - jnp.log1p(-a0)
    w_out = jax.random.normal(ks[9], (L, D_MODEL, D_MODEL), f32) * D_MODEL ** -0.5 * DEEPNORM_BETA
    ln1_g = 1.0 + 0.02 * jax.random.normal(ks[10], (L, D_MODEL), f32)
    ln1_b = 0.02 * jax.random.normal(ks[11], (L, D_MODEL), f32)
    w_up = jax.random.normal(ks[12], (L, D_MODEL, D_FF), f32) * D_MODEL ** -0.5 * DEEPNORM_BETA
    b_up = 0.02 * jax.random.normal(ks[13], (L, D_FF), f32)
    w_down = jax.random.normal(ks[14], (L, D_FF, D_MODEL), f32) * D_FF ** -0.5 * DEEPNORM_BETA
    b_down = 0.02 * jax.random.normal(ks[15], (L, D_MODEL), f32)
    ln2_g = 1.0 + 0.02 * jax.random.normal(ks[16], (L, D_MODEL), f32)
    ln2_b = 0.02 * jax.random.normal(ks[17], (L, D_MODEL), f32)
    x = jax.random.normal(ks[0], (BATCH, SEQ, D_MODEL), f32)
    return {"x": x, "w_in": w_in, "conv_w": conv_w, "conv_b": conv_b,
            "w_rg": w_rg, "b_rg": b_rg, "w_ig": w_ig, "b_ig": b_ig,
            "lru_lambda": lru_lambda, "w_out": w_out, "ln1_g": ln1_g, "ln1_b": ln1_b,
            "w_up": w_up, "b_up": b_up, "w_down": w_down, "b_down": b_down,
            "ln2_g": ln2_g, "ln2_b": ln2_b}

def reference(x, w_in, conv_w, conv_b, w_rg, b_rg, w_ig, b_ig, lru_lambda, w_out,
              ln1_g, ln1_b, w_up, b_up, w_down, b_down, ln2_g, ln2_b):
    B, S, _ = x.shape
    for l in range(DEPTH):
        proj = jnp.einsum('bsd,de->bse', x, w_in[l])
        q, k, v, xr, gr = jnp.split(
            proj, [ATTN_WIDTH, 2 * ATTN_WIDTH, 3 * ATTN_WIDTH, 3 * ATTN_WIDTH + LRU_WIDTH], axis=-1)
        hs = (B, S, N_ATTN_HEADS, HEAD_DIM)
        attn = moba_attention(q.reshape(hs), k.reshape(hs), v.reshape(hs))
        xr = causal_depthwise_conv(xr, conv_w[l], conv_b[l])
        lru = rg_lru(xr, w_rg[l], b_rg[l], w_ig[l], b_ig[l], lru_lambda[l]) * jax.nn.gelu(gr)
        mix = jnp.einsum('bse,ed->bsd', jnp.concatenate([attn, lru], axis=-1), w_out[l])
        x = layer_norm(DEEPNORM_ALPHA * x + mix, ln1_g[l], ln1_b[l])
        h = jnp.square(jax.nn.relu(jnp.einsum('bsd,df->bsf', x, w_up[l]) + b_up[l]))
        h = jnp.einsum('bsf,fd->bsd', h, w_down[l]) + b_down[l]
        x = layer_norm(DEEPNORM_ALPHA * x + h, ln2_g[l], ln2_b[l])
    return x


_drawn_inputs = setup_inputs


def setup_inputs(seed=0):
    import zlib

    import numpy as np

    out = dict(_drawn_inputs(seed))
    spreads = {}
    factors = {'conv_b': 3.399,
     'b_rg': 64.0,
     'b_ig': 49.807,
     'ln1_g': 8.094,
     'ln1_b': 7.996,
     'b_up': 7.023,
     'b_down': 55.553,
     'ln2_g': 23.304,
     'ln2_b': 23.485}
    for name, (base, spread) in spreads.items():
        noise = np.random.default_rng([zlib.crc32(name.encode()), seed]).standard_normal(out[name].shape)
        drawn = base * np.exp(spread * noise) if base else spread * noise
        out[name] = __import__('jax').numpy.asarray(drawn.astype(out[name].dtype))
    for name, factor in factors.items():
        out[name] = (out[name] * factor).astype(out[name].dtype)
    return out
```

```python
from contextlib import ExitStack

import concourse.bass as bass
from concourse import mybir

F32 = mybir.dt.float32
F32R = mybir.dt.float32r
ACT = mybir.ActivationFunctionType
ALU = mybir.AluOpType
AX = mybir.AxisListType

P = 128
BANK = 512
RING = 4
UNIT = 2048
NEG = -1e30
LN_EPS = 1e-5


def hybrid_layer(nc, x, w_in, conv_w, conv_b, w_rg, b_rg, w_ig, b_ig, lru_lambda, w_out,
                 ln1_g, ln1_b, w_up, b_up, w_down, b_down, ln2_g, ln2_b, out):
    _, SEQ, D = x.shape
    DEPTH = w_in.shape[0]
    ST = SEQ // P
    KT = D // P
    LRU_W = conv_w.shape[2]
    JT = LRU_W // P
    TAPS = conv_w.shape[1]
    ATT_W = D - LRU_W
    BLK = w_rg.shape[2]
    HEADS = 8
    DH = ATT_W // HEADS
    FF = w_up.shape[2]
    GROUPS = FF // 512
    FG = 4
    HALF = 512
    ALPHA = (2.0 * DEPTH) ** 0.25
    SCALE = DH ** -0.5
    SLOPES = [2.0 ** (-8.0 * (h + 1) / HEADS) for h in range(HEADS)]
    assert DEPTH == 1 and ST == 2 and KT == 8 and JT == 4 and ATT_W == 512 and GROUPS == 8 and TAPS == 4

    K0, V0, XR0, GR0 = ATT_W, 2 * ATT_W, 3 * ATT_W, 3 * ATT_W + LRU_W
    UNIT_COLS = [XR0, XR0 + 256, GR0, GR0 + 256, V0, V0 + 256, K0, 0, K0 + 256, 256]
    TILES = ([("xr", j) for j in range(4)] + [("gr", j) for j in range(4)]
             + [("v", j) for j in range(4)] + [("k", 0), ("k", 1), ("q", 0), ("q", 1)]
             + [("k", 2), ("k", 3), ("q", 2), ("q", 3)])
    N_IN = len(UNIT_COLS)
    N_OUT0 = N_IN
    N_UP0 = N_OUT0 + 4
    OUT_ROWS = [ATT_W, ATT_W + 256, 0, 256]

    def unit_u(g):
        return 4 * g + 12

    def unit_d(g):
        return 4 * g + 18

    LAST_D = 4 * (GROUPS - 1) + 16

    C_CW, C_CB, C_BR, C_BI, C_LAM, C_BUP = 0, 16, 20, 24, 28, 32
    N_PAR = C_BUP + FF // P

    with ExitStack() as ctx:
        def sb(name, shape, dt=F32):
            return ctx.enter_context(nc.sbuf_tensor(name, shape, dt))

        def sem(name):
            return ctx.enter_context(nc.semaphore(name))

        w_raw = sb("w_raw", [P, RING, UNIT])
        w_hi = sb("w_hi", [P, RING, UNIT], F32R)
        w_lo = sb("w_lo", [P, RING, UNIT], F32R)
        xs = sb("xs", [P, ST, D])
        xt_hi = sb("xt_hi", [P, KT, SEQ], F32R)
        xt_lo = sb("xt_lo", [P, KT, SEQ], F32R)
        cat_hi = sb("cat_hi", [P, KT, SEQ], F32R)
        cat_lo = sb("cat_lo", [P, KT, SEQ], F32R)
        ht_hi = sb("ht_hi", [P, 2, FG, SEQ], F32R)
        ht_lo = sb("ht_lo", [P, 2, FG, SEQ], F32R)
        ln1 = sb("ln1", [P, 2, D])
        XRP = SEQ + TAPS - 1
        area = sb("area", [P, JT * XRP + 5 * JT * SEQ])
        xrp = area[:, 0:JT * XRP].rearrange("p (j c) -> p j c", j=JT)

        def lru_part(n):
            a = JT * XRP + n * JT * SEQ
            return area[:, a:a + JT * SEQ]

        root = area[:, 0:JT * SEQ]
        xc, gate_r, gate_i, decay, gelu = (lru_part(n) for n in range(5))
        ln2 = area[:, 0:2 * D].rearrange("p (n d) -> p n d", n=2)
        b_dn = area[:, 2 * D:3 * D]
        relu_h = area[:, 3 * D:4 * D].rearrange("p (n d) -> p n d", n=2)
        sq_h = area[:, 4 * D:5 * D].rearrange("p (n d) -> p n d", n=2)
        qt = sb("qt", [P, JT, SEQ])
        kt = sb("kt", [P, JT, SEQ])
        vs = sb("vs", [P, ST, ATT_W])
        NB = 3 * P
        att = sb("att", [P, 4, NB])
        prob = att[:, 0:2, :]
        prob_t = att[:, 2:4, :]
        gate_w = att[:, :, :].rearrange("p a b -> p (a b)")[:, 0:2 * JT * P].rearrange(
            "p (g j c) -> p g j c", g=2, j=JT)
        o_nat = sb("o_nat", [P, ST, 256])
        alibi = sb("alibi", [P, NB])
        ident = sb("ident", [P, P])
        rows = sb("rows", [N_PAR, P])
        par = sb("par", [P, N_PAR])
        sp = sb("sp", [P, 10, 4])
        maxes = sb("maxes", [P, 2 * HEADS])
        sums = sb("sums", [P, 2, ST, 4])
        rsums = sb("rsums", [P, 2, ST, 4])
        stats = sb("stats", [P, ST, 2, 6])
        mv = sb("mv", [P, ST, 4])
        eps = sb("eps", [P, 1])

        bank = [ctx.enter_context(nc.psum_tensor(f"bank{n}", [P, BANK], F32)) for n in range(8)]

        x_in = [sem(f"x_in{s}") for s in range(ST)]
        raw_in = [sem(f"raw_in{n}") for n in range(RING)]
        par_in, ln1_in, ln2_in, gw_in = sem("par_in"), sem("ln1_in"), sem("ln2_in"), sem("gw_in")
        out_done = sem("out_done")
        const_ok = sem("const_ok")
        pool_step = sem("pool_step")
        hi_ok, lo_ok = sem("hi_ok"), sem("lo_ok")
        par_t, par_ok, sp_z, sp_step, sp_ok = (sem("par_t"), sem("par_ok"), sem("sp_z"), sem("sp_step"),
                                               sem("sp_ok"))
        xt_t, xt_hi_ok, xt_lo_ok = sem("xt_t"), sem("xt_hi_ok"), sem("xt_lo_ok")
        proj_ok, proj_out = sem("proj_ok"), sem("proj_out")
        conv_step, conv_ok = sem("conv_step"), sem("conv_ok")
        gates_ok, gates_out = sem("gates_ok"), sem("gates_out")
        tanh_ok, decay_ok, decay2_ok = sem("tanh_ok"), sem("decay_ok"), sem("decay2_ok")
        root2_ok, root_ok, ix_ok, u_ok = sem("root2_ok"), sem("root_ok"), sem("ix_ok"), sem("u_ok")
        scan_ok, lru_ok, lru_hi, lru_lo = sem("scan_ok"), sem("lru_ok"), sem("lru_hi"), sem("lru_lo")
        score_ok, logit_ok, max_ok, prob_ok = sem("score_ok"), sem("logit_ok"), sem("max_ok"), sem("prob_ok")
        max_half = sem("max_half")
        pt_ok, pt_out, pv_ok = sem("pt_ok"), sem("pt_out"), sem("pv_ok")
        rsum_ok, norm_ok, ot_ok, ot_hi, ot_lo = (sem("rsum_ok"), sem("norm_ok"), sem("ot_ok"), sem("ot_hi"),
                                                 sem("ot_lo"))
        mix_ok, mix_part, res_ok, ln_step = sem("mix_ok"), sem("mix_part"), sem("res_ok"), sem("ln_step")
        mv_ok, dev_ok, rdev_ok, x1_ok = sem("mv_ok"), sem("dev_ok"), sem("rdev_ok"), sem("x1_ok")
        up_ok, relu_ok, sq_ok, hhi_ok, hlo_ok = (sem("up_ok"), sem("relu_ok"), sem("sq_ok"), sem("hhi_ok"),
                                                 sem("hlo_ok"))
        down_ok, res2_ok, y_ok, out_ok = sem("down_ok"), sem("res2_ok"), sem("y_ok"), sem("out_ok")

        w_in_k = w_in[0].rearrange("(k p) c -> p k c", p=P)
        w_up_k = w_up[0].rearrange("(k p) c -> p k c", p=P)
        w_out_k = w_out[0].rearrange("(k p) c -> p k c", p=P)
        w_dn_k = w_down[0].rearrange("(k p) c -> p k c", p=P)

        def cols8(ring, slot):
            return ring[:, slot, :].rearrange("p (k c) -> p k c", k=8)

        def rows2(ring, slot):
            return ring[:, slot, :].rearrange("p (k c) -> p k c", k=2)

        block = ctx.enter_context(nc.Block())

        @block.sync
        def _(sp_e):
            for s in range(ST):
                sp_e.dma_start(xs[:, s, :], x[0, s * P:(s + 1) * P, :]).then_inc(x_in[s], 16)

            for n, c in enumerate(UNIT_COLS):
                if n >= RING:
                    sp_e.wait_ge(lo_ok, n - RING + 1)
                sp_e.dma_start(cols8(w_raw, n % RING), w_in_k[:, :, c:c + 256]).then_inc(raw_in[n % RING], 16)
            for m, r in enumerate(OUT_ROWS):
                n = N_OUT0 + m
                sp_e.wait_ge(lo_ok, n - RING + 1)
                sp_e.dma_start(rows2(w_raw, n % RING),
                               w_out_k[:, r // P:r // P + 2, :]).then_inc(raw_in[n % RING], 16)

            def load_up(g, n):
                for m in range(2):
                    slot = (2 if isinstance(g, int) and g == 0 else 0) + m
                    sp_e.wait_ge(lo_ok, n + m - RING + 1)
                    sp_e.dma_start(cols8(w_raw, slot),
                                   w_up_k[:, :, bass.ds(g * 512 + m * 256, 256)]).then_inc(raw_in[slot], 16)

            def load_down(g, n, slot=2):
                for m in range(2):
                    sp_e.wait_ge(lo_ok, n + m - RING + 1)
                    sp_e.dma_start(rows2(w_raw, slot + m),
                                   w_dn_k[:, bass.ds(g * 4 + 2 * m, 2), :]).then_inc(raw_in[slot + m], 16)

            load_up(0, N_UP0)
            load_up(1, N_UP0 + 2)
            load_down(0, unit_d(0))
            with sp_e.Fori(1, GROUPS - 1) as g:
                load_up(g + 1, unit_u(g + 1))
                load_down(g, unit_d(g))
            load_down(GROUPS - 1, LAST_D, 0)
            for s in range(ST):
                for n in range(2):
                    sp_e.wait_ge(out_ok, 2 * s + n + 1)
                    sp_e.dma_start(out[0, s * P:(s + 1) * P, n * HALF:(n + 1) * HALF],
                                   xs[:, s, n * HALF:(n + 1) * HALF]).then_inc(out_done, 16)
            sp_e.wait_ge(out_done, 16 * 2 * ST)

        @block.gpsimd
        def _(pool):
            nc.gpsimd.memset(ident[:], 0.0).then_inc(pool_step, 1)
            pool.wait_ge(pool_step, 1)
            nc.gpsimd.affine_select(out=ident[:], in_=ident[:], compare_op=ALU.not_equal, fill=1.0, base=0,
                                    pattern=[[-1, P]], channel_multiplier=1).then_inc(const_ok, 1)
            nc.gpsimd.memset(xrp[:, :, 0:TAPS - 1], 0.0).then_inc(const_ok, 1)
            nc.gpsimd.memset(eps[:], LN_EPS).then_inc(const_ok, 1)
            nc.gpsimd.memset(gate_w, 0.0).then_inc(pool_step, 1)
            pool.wait_ge(pool_step, 2)
            for n, w in enumerate((w_rg, w_ig)):
                blocks = w[0].rearrange("(j h) e f -> h e j f", h=2)
                for h in range(2):
                    pool.dma_start(gate_w[h * BLK:(h + 1) * BLK, n, :, h * BLK:(h + 1) * BLK],
                                   blocks[h]).then_inc(gw_in, 16)
            nc.gpsimd.iota(alibi[:, 0:P], [[1, P]], base=0, channel_multiplier=-1,
                           allow_small_or_imprecise_dtypes=True).then_inc(pool_step, 1)
            nc.gpsimd.iota(alibi[:, P:NB], [[1, 2 * P]], base=-P, channel_multiplier=-1,
                           allow_small_or_imprecise_dtypes=True).then_inc(pool_step, 1)
            pool.wait_ge(pool_step, 4)
            nc.gpsimd.affine_select(out=alibi[:, 0:P], in_=alibi[:, 0:P], compare_op=ALU.is_ge, fill=NEG,
                                    base=0, pattern=[[-1, P]], channel_multiplier=1).then_inc(const_ok, 1)
            nc.gpsimd.affine_select(out=alibi[:, P:NB], in_=alibi[:, P:NB], compare_op=ALU.is_ge, fill=NEG,
                                    base=P, pattern=[[-1, 2 * P]], channel_multiplier=1).then_inc(const_ok, 1)
            for n, v in enumerate((ln1_g, ln1_b)):
                pool.dma_start(ln1[:, n, :], v[0:1, :].to_broadcast([P, D])).then_inc(ln1_in, 16)
            pool.wait_ge(lru_lo, 1)
            for dst, v in ((ln2[:, 0, :], ln2_g), (ln2[:, 1, :], ln2_b), (b_dn, b_down)):
                pool.dma_start(dst, v[0:1, :].to_broadcast([P, D])).then_inc(ln2_in, 16)

        @block.tensor
        def _(pe):
            def mm3(dst, a_hi, a_lo, b_hi, b_lo, start, stop):
                pe.matmul(dst, a_hi, b_hi, start=start, stop=False)
                pe.matmul(dst, a_hi, b_lo, start=False, stop=False)
                return pe.matmul(dst, a_lo, b_hi, start=False, stop=stop)

            def transpose_x(n, to):
                s, half = n // 2, n % 2
                for q in range(4):
                    c = (4 * half + q) * P
                    t = pe.transpose(to[:, q * P:(q + 1) * P], xs[:, s, c:c + P], ident[:])
                t.then_inc(xt_t, 1)

            pe.wait_ge(const_ok, 1)
            for n in range(4):
                if n % 2 == 0:
                    pe.wait_ge(x_in[n // 2], 16)
                transpose_x(n, bank[4 + n])
            pe.wait_ge(par_in, 6 * 16)
            pe.transpose(bank[3][:, 0:N_PAR], rows[:, :], ident[0:N_PAR, 0:N_PAR]).then_inc(par_t, 1)

            def proj(n):
                kind, j = TILES[n]
                u = n // 2
                slot = u % RING
                hi, lo = cols8(w_hi, slot), cols8(w_lo, slot)
                dst = bank[n % 3][:, 0:256]
                pe.wait_ge(lo_ok, u + 1)
                if n >= 3:
                    pe.wait_ge(proj_out, n - 2)
                for k in range(KT):
                    first, last = k == 0, k == KT - 1
                    if kind == "v":
                        s = slice((n % 2) * P, (n % 2 + 1) * P)
                        i = mm3(dst, xt_hi[:, k, s], xt_lo[:, k, s], hi[:, k, :], lo[:, k, :], first, last)
                    else:
                        c = slice((n % 2) * P, (n % 2 + 1) * P)
                        i = mm3(dst, hi[:, k, c], lo[:, k, c], xt_hi[:, k, :], xt_lo[:, k, :], first, last)
                i.then_inc(proj_ok, 1)

            def gates():
                pe.wait_ge(gw_in, 4 * 16)
                for j in range(JT):
                    pe.wait_ge(conv_ok, j + 1)
                    for n in range(2):
                        i = pe.matmul(bank[3 + j][:, n * SEQ:(n + 1) * SEQ], gate_w[:, n, j, :],
                                      xc[:, j * SEQ:(j + 1) * SEQ], start=True, stop=True)
                    i.then_inc(gates_ok, 1)

            def scores(h):
                b, j, r = bank[4 + h % 2], h // 2, slice(DH * (h % 2), DH * (h % 2) + DH)
                if h == 0:
                    pe.wait_ge(gates_out, 2 * JT)
                pe.wait_ge(proj_out, 16 if h < 4 else 20)
                if h >= 2:
                    pe.wait_ge(logit_ok, h - 1)
                pe.matmul(b[:, 0:P], qt[r, j, 0:P], kt[r, j, 0:P], start=True, stop=True)
                pe.matmul(b[:, P:NB], qt[r, j, P:SEQ], kt[r, j, :], start=True, stop=True).then_inc(score_ok, 1)

            def turn_prob(h):
                pe.wait_ge(prob_ok, 2 * (h + 1))
                if h >= 1:
                    pe.wait_ge(pt_out, h)
                for q in range(3):
                    t = pe.transpose(bank[7][:, q * P:(q + 1) * P], prob[:, h % 2, q * P:(q + 1) * P], ident[:])
                t.then_inc(pt_ok, 1)

            def values(h):
                pe.wait_ge(pt_out, h + 1)
                if h == 4:
                    pe.wait_ge(norm_ok, 1)
                v = slice(h * DH, (h + 1) * DH)
                c = (h % 4) * DH
                pt = prob_t[:, h % 2, :]
                pe.matmul(bank[6][:, c:c + DH], pt[:, 0:P], vs[:, 0, v], start=True, stop=True)
                pe.matmul(bank[6][:, 256 + c:256 + c + DH], pt[:, P:2 * P], vs[:, 0, v], start=True, stop=False)
                pe.matmul(bank[6][:, 256 + c:256 + c + DH], pt[:, 2 * P:NB], vs[:, 1, v],
                          start=False, stop=True).then_inc(pv_ok, 1)

            def turn_out(part):
                b = bank[3] if part == 0 else bank[7]
                pe.wait_ge(norm_ok, part + 1)
                if part == 1:
                    pe.wait_ge(pt_out, HEADS)
                for k in range(2):
                    for s in range(ST):
                        t = pe.transpose(b[:, k * SEQ + s * P:k * SEQ + (s + 1) * P],
                                         o_nat[:, s, k * P:(k + 1) * P], ident[:])
                t.then_inc(ot_ok, 1)

            def mix(s, n, part):
                units = {0: (10, 11), 1: (12,), 2: (13,)}[part]
                rows_at = {0: 4, 1: 0, 2: 2}[part]
                if part == 0:
                    pe.wait_ge(lru_lo, 1)
                    pe.wait_ge(proj_out, 20)
                    if s == 1 and n == 1:
                        pe.wait_ge(ot_lo, 1)
                else:
                    pe.wait_ge(ot_lo, part)
                for a, u in enumerate(units):
                    pe.wait_ge(lo_ok, u + 1)
                    for b in range(2):
                        k = rows_at + 2 * a + b
                        c = slice(n * HALF, (n + 1) * HALF)
                        i = mm3(bank[2 * s + n][:, :], cat_hi[:, k, s * P:(s + 1) * P],
                                cat_lo[:, k, s * P:(s + 1) * P], rows2(w_hi, u % RING)[:, b, c],
                                rows2(w_lo, u % RING)[:, b, c], k == 4, k == 3)
                if part == 2:
                    i.then_inc(mix_ok, 1)
                elif s == 1 and n == 1:
                    i.then_inc(mix_part, 1)

            for n in range(7):
                if n == 0:
                    pe.wait_ge(xt_lo_ok, 4)
                proj(n)
            gates()
            for n in range(7, 16):
                proj(n)
            pe.wait_ge(const_ok, 5)
            scores(0)
            scores(1)
            proj(16)
            turn_prob(0)
            scores(2)
            proj(17)
            values(0)
            turn_prob(1)
            scores(3)
            proj(18)
            values(1)
            turn_prob(2)
            proj(19)
            values(2)
            turn_prob(3)
            scores(4)
            scores(5)
            mix(0, 0, 0)
            values(3)
            turn_prob(4)
            scores(6)
            mix(0, 1, 0)
            turn_out(0)
            values(4)
            turn_prob(5)
            scores(7)
            mix(0, 0, 1)
            values(5)
            turn_prob(6)
            mix(0, 1, 1)
            values(6)
            turn_prob(7)
            mix(1, 0, 0)
            values(7)
            mix(1, 1, 0)
            turn_out(1)
            mix(0, 0, 2)
            mix(0, 1, 2)
            mix(1, 0, 1)
            mix(1, 1, 1)
            mix(1, 0, 2)
            mix(1, 1, 2)

            def up(g, n, s_range, ups_done):
                par2 = ups_done % 2
                base = (2 if (isinstance(g, int) and g == 0) else 0)
                cols = slice(s_range[0] * P, (s_range[-1] + 1) * P)
                for m in range(2):
                    slot = base + m
                    hi, lo = cols8(w_hi, slot), cols8(w_lo, slot)
                    pe.wait_ge(lo_ok, n + m + 1)
                    b = bank[4 + 2 * par2 + m]
                    if not (isinstance(g, int) and g < 2):
                        pe.wait_ge(relu_ok, 4 * g - 6 + 2 * m)
                    for f in range(2):
                        dst = b[:, f * SEQ + cols.start:f * SEQ + cols.stop]
                        for k in range(KT):
                            i = mm3(dst, hi[:, k, f * P:(f + 1) * P], lo[:, k, f * P:(f + 1) * P],
                                    xt_hi[:, k, cols], xt_lo[:, k, cols], k == 0, k == KT - 1)
                    if s_range[-1] == ST - 1:
                        i.then_inc(up_ok, 1)

            def down(g, par2, first=False, last=False):
                slot = 0 if last else 2
                pe.wait_ge(hlo_ok, 2 * g + 2)
                pe.wait_ge(lo_ok, (LAST_D if last else unit_d(g)) + 2)
                for s in range(ST):
                    for n in range(2):
                        c = slice(n * HALF, (n + 1) * HALF)
                        for f in range(FG):
                            i = mm3(bank[2 * s + n][:, :], ht_hi[:, par2, f, s * P:(s + 1) * P],
                                    ht_lo[:, par2, f, s * P:(s + 1) * P], rows2(w_hi, slot + f // 2)[:, f % 2, c],
                                    rows2(w_lo, slot + f // 2)[:, f % 2, c], first and f == 0, last and f == FG - 1)
                        if last:
                            i.then_inc(y_ok, 1)
                if not last:
                    i.then_inc(down_ok, 1)

            pe.wait_ge(norm_ok, 2)
            pe.wait_ge(ot_lo, 2)
            for n in range(2):
                pe.wait_ge(x1_ok, n + 1)
                transpose_x(n, bank[6 + n])
            pe.wait_ge(xt_lo_ok, 6)
            up(0, N_UP0, [0], 0)
            for n in range(2, 4):
                pe.wait_ge(x1_ok, n + 1)
                transpose_x(n, bank[n - 2])
            up(1, N_UP0 + 2, [0], 1)
            pe.wait_ge(xt_lo_ok, 8)
            up(0, N_UP0, [1], 0)
            up(1, N_UP0 + 2, [1], 1)
            pe.wait_ge(res_ok, 4)
            down(0, 0, first=True)
            with pe.Fori(1, GROUPS - 1, 2) as g:
                for q in range(2):
                    up(g + q + 1, unit_u(g + q + 1), [0, 1], q)
                    down(g + q, 1 - q)
            down(GROUPS - 1, 1, last=True)

        @block.scalar
        def _(act):
            A = nc.scalar.activation
            for c, v in ((C_CW, conv_w), (C_CB, conv_b), (C_BR, b_rg), (C_BI, b_ig), (C_LAM, lru_lambda),
                         (C_BUP, b_up)):
                src = (v.rearrange("l t (j p) -> (l t j) p", p=P) if len(v.shape) == 3
                       else v.rearrange("l (j p) -> (l j) p", p=P))
                act.dma_start(rows[c:c + src.shape[0], :], src).then_inc(par_in, 16)

            def x_hi(n, src):
                s, half = (n // 2) % 2, n % 2
                act.wait_ge(xt_t, n + 1)
                nc.scalar.copy(xt_hi[:, 4 * half:4 * half + 4, s * P:(s + 1) * P],
                               src[:, :].rearrange("p (k c) -> p k c", k=4)).then_inc(xt_hi_ok, 1)

            def unit_hi(slot, nth, user, uses):
                act.wait_ge(raw_in[slot], 16 * nth)
                if user is not None:
                    act.wait_ge(user, uses)
                nc.scalar.copy(w_hi[:, slot, :], w_raw[:, slot, :]).then_inc(hi_ok, 1)

            def u_hi(n):
                if n < RING:
                    user, uses = None, 0
                elif n < RING + N_IN:
                    user, uses = proj_ok, 2 * (n - RING + 1)
                else:
                    user, uses = ((mix_part, 1), (mix_part, 1), (mix_part, 2), (mix_ok, 4))[n - N_UP0]
                unit_hi(n % RING, n // RING + 1, user, uses)

            def proj_evict(n):
                kind, j = TILES[n]
                src = bank[n % 3][:, 0:256]
                act.wait_ge(proj_ok, n + 1)
                if kind == "xr":
                    i = nc.scalar.copy(xrp[:, j, TAPS - 1:], src)
                elif kind == "gr":
                    i = A(gelu[:, j * SEQ:(j + 1) * SEQ], src, ACT.Gelu_apprx_tanh)
                elif kind == "v":
                    i = nc.scalar.copy(vs[:, j % 2, (j // 2) * 256:(j // 2 + 1) * 256], src)
                elif kind == "k":
                    i = nc.scalar.copy(kt[:, j, :], src)
                else:
                    i = nc.scalar.mul(qt[:, j, :], src, SCALE)
                i.then_inc(proj_out, 1)

            def exps(h):
                act.wait_ge(max_ok, h + 1)
                for s, c in ((0, slice(0, P)), (1, slice(P, NB))):
                    A(prob[:, h % 2, c], prob[:, h % 2, c], ACT.Exp, bias=maxes[:, 2 * h + s:2 * h + s + 1],
                      accum_out=sums[:, h // 4, s, h % 4:h % 4 + 1]).then_inc(prob_ok, 1)

            def out_hi(part):
                b = bank[3] if part == 0 else bank[7]
                act.wait_ge(ot_ok, part + 1)
                nc.scalar.copy(cat_hi[:, 2 * part:2 * part + 2, :],
                               b[:, :].rearrange("p (k c) -> p k c", k=2)).then_inc(ot_hi, 1)

            for n in range(4):
                x_hi(n, bank[4 + n])
            u_hi(0)
            act.wait_ge(sp_step, 2)
            A(sp[:, 1, :], sp[:, 0, :], ACT.Exp, scale=-1.0).then_inc(sp_z, 1)
            u_hi(1)
            u_hi(2)
            act.wait_ge(const_ok, 2)
            proj_evict(0)
            u_hi(3)
            proj_evict(1)
            u_hi(4)
            for n in range(2, 8):
                proj_evict(n)
                if n % 2:
                    u_hi(n // 2 + 4)
            for j in range(JT):
                act.wait_ge(gates_ok, j + 1)
                for n, (dst, c) in enumerate(((gate_r, C_BR), (gate_i, C_BI))):
                    A(dst[:, j * SEQ:(j + 1) * SEQ], bank[3 + j][:, n * SEQ:(n + 1) * SEQ], ACT.Sigmoid,
                      bias=par[:, c + j:c + j + 1]).then_inc(gates_out, 1)
            proj_evict(8)
            proj_evict(9)
            u_hi(8)
            act.wait_ge(sp_ok, 2)
            act.wait_ge(gates_out, 2 * JT)
            act.wait_ge(conv_ok, JT)
            for j in range(JT):
                c = slice(j * SEQ, (j + 1) * SEQ)
                A(root[:, c], gate_r[:, c], ACT.Tanh, scale=sp[:, 8, j:j + 1]).then_inc(tanh_ok, 1)
            for j in range(JT):
                c = slice(j * SEQ, (j + 1) * SEQ)
                A(decay[:, c], gate_r[:, c], ACT.Exp, scale=sp[:, 9, j:j + 1]).then_inc(decay_ok, 1)
            proj_evict(10)
            act.wait_ge(decay_ok, JT)
            act.wait_ge(tanh_ok, JT)
            A(gate_r, decay, ACT.Square).then_inc(decay2_ok, 1)
            proj_evict(11)
            u_hi(9)
            act.wait_ge(root2_ok, 1)
            A(root, root, ACT.Sqrt).then_inc(root_ok, 1)
            proj_evict(12)
            proj_evict(13)
            u_hi(10)
            proj_evict(14)
            proj_evict(15)
            u_hi(11)
            act.wait_ge(lru_ok, 1)
            nc.scalar.copy(cat_hi[:, 4:8, :], gelu.rearrange("p (k c) -> p k c", k=4)).then_inc(lru_hi, 1)
            exps(0)
            exps(1)
            proj_evict(16)
            exps(2)
            proj_evict(17)
            u_hi(12)
            exps(3)
            proj_evict(18)
            proj_evict(19)
            u_hi(13)
            exps(4)
            exps(5)
            exps(6)
            out_hi(0)
            exps(7)
            out_hi(1)
            u_hi(14)

            def deviation(i, s):
                act.wait_ge(mv_ok, i + 1)
                A(mv[:, s, 2:3], mv[:, s, 1:2], ACT.Sqrt, bias=eps[:]).then_inc(dev_ok, 1)

            deviation(0, 0)
            x_hi(4, bank[6])
            x_hi(5, bank[7])
            u_hi(15)
            u_hi(16)
            deviation(1, 1)
            x_hi(6, bank[0])
            x_hi(7, bank[1])
            u_hi(17)
            act.wait_ge(ln2_in, 3 * 16)

            def hidden(g, par2, m):
                pe_pair = 2 * g + m
                act.wait_ge(up_ok, pe_pair + 1)
                if not (isinstance(g, int) and g == 0):
                    act.wait_ge(hlo_ok, pe_pair - 1)
                for f in range(2):
                    A(relu_h[:, m, f * SEQ:(f + 1) * SEQ], bank[4 + 2 * par2 + m][:, f * SEQ:(f + 1) * SEQ],
                      ACT.Relu, bias=par[:, bass.ds(C_BUP + 4 * g + 2 * m + f, 1)]).then_inc(relu_ok, 1)
                act.wait_ge(relu_ok, 2 * pe_pair + 2)
                A(ht_hi[:, par2, 2 * m:2 * m + 2, :], relu_h[:, m, :].rearrange("p (k c) -> p k c", k=2),
                  ACT.Square).then_inc(hhi_ok, 1)

            def down_hi(g, first=False):
                for m in range(2):
                    unit_hi(2 + m, g + 5, *((up_ok, m + 1) if first else (down_ok, g)))

            hidden(0, 0, 0)
            hidden(0, 0, 1)
            down_hi(0, first=True)
            with act.Fori(1, GROUPS - 1, 2) as g:
                for q in range(2):
                    for m in range(2):
                        hidden(g + q, 1 - q, m)
                        unit_hi(m, g + q + 5, up_ok, 2 * (g + q) + m + 1)
                    down_hi(g + q)
            hidden(GROUPS - 1, 1, 0)
            hidden(GROUPS - 1, 1, 1)
            for m in range(2):
                unit_hi(m, GROUPS + 4, up_ok, 2 * (GROUPS - 1) + m + 1)
            deviation(2, 0)
            deviation(3, 1)

        @block.vector
        def _(dve):
            V = nc.vector

            def x_lo(n, src):
                s, half = (n // 2) % 2, n % 2
                dst = (slice(None), slice(4 * half, 4 * half + 4), slice(s * P, (s + 1) * P))
                dve.wait_ge(xt_hi_ok, n + 1)
                V.tensor_tensor(xt_lo[dst], src[:, :].rearrange("p (k c) -> p k c", k=4),
                                xt_hi[dst].bitcast(F32), ALU.subtract).then_inc(xt_lo_ok, 1)

            def unit_lo(n, slot):
                dve.wait_ge(hi_ok, n + 1)
                V.tensor_tensor(w_lo[:, slot, :], w_raw[:, slot, :], w_hi[:, slot, :].bitcast(F32),
                                ALU.subtract).then_inc(lo_ok, 1)

            def u_lo(n):
                unit_lo(n, n % RING)

            for n in range(4):
                x_lo(n, bank[4 + n])
            u_lo(0)

            steps = [0]

            def step(i):
                steps[0] += 1
                i.then_inc(sp_step, 1)
                dve.wait_ge(sp_step, steps[0])

            dve.wait_ge(par_t, 1)
            V.tensor_copy(par[:], bank[3][:, 0:N_PAR]).then_inc(par_ok, 1)
            dve.wait_ge(par_ok, 1)
            lam = par[:, C_LAM:C_LAM + 4]
            step(V.tensor_scalar(sp[:, 2, :], lam, -1.0, None, ALU.mult))
            step(V.tensor_tensor(sp[:, 0, :], lam, sp[:, 2, :], ALU.max))
            dve.wait_ge(sp_z, 1)
            step(V.tensor_scalar(sp[:, 3, :], sp[:, 1, :], 2.0, None, ALU.add))
            step(V.reciprocal(sp[:, 4, :], sp[:, 3, :]))
            step(V.tensor_tensor(sp[:, 5, :], sp[:, 1, :], sp[:, 4, :], ALU.mult))
            step(V.tensor_tensor(sp[:, 6, :], sp[:, 5, :], sp[:, 5, :], ALU.mult))
            step(V.tensor_scalar(sp[:, 7, :], sp[:, 6, :], 1.0 / 15, None, ALU.mult))
            for c in (13, 11, 9, 7, 5, 3):
                step(V.scalar_tensor_tensor(sp[:, 7, :], sp[:, 7, :], 1.0 / c, sp[:, 6, :], ALU.add, ALU.mult))
            step(V.scalar_tensor_tensor(sp[:, 7, :], sp[:, 7, :], 1.0, sp[:, 5, :], ALU.add, ALU.mult))
            step(V.tensor_scalar(sp[:, 2, :], sp[:, 2, :], 0.0, 8.0, ALU.max, ALU.mult))
            V.scalar_tensor_tensor(sp[:, 8, :], sp[:, 7, :], 16.0, sp[:, 2, :], ALU.mult, ALU.add).then_inc(sp_ok, 1)
            dve.wait_ge(sp_ok, 1)
            V.tensor_scalar(sp[:, 9, :], sp[:, 8, :], -1.0, None, ALU.mult).then_inc(sp_ok, 1)
            u_lo(1)
            u_lo(2)

            def conv(j):
                dst = xc[:, j * SEQ:(j + 1) * SEQ]
                dve.wait_ge(proj_out, j + 1)
                V.tensor_scalar(dst, xrp[:, j, 0:SEQ], par[:, C_CW + j:C_CW + j + 1],
                                par[:, C_CB + j:C_CB + j + 1], ALU.mult, ALU.add).then_inc(conv_step, 1)
                for t in range(1, TAPS):
                    dve.wait_ge(conv_step, 3 * j + t)
                    c = C_CW + JT * t + j
                    V.scalar_tensor_tensor(dst, xrp[:, j, t:t + SEQ], par[:, c:c + 1], dst, ALU.mult,
                                           ALU.add).then_inc(conv_ok if t == TAPS - 1 else conv_step, 1)

            dve.wait_ge(const_ok, 2)
            conv(0)
            u_lo(3)
            conv(1)
            u_lo(4)
            conv(2)
            conv(3)
            u_lo(5)
            u_lo(6)
            u_lo(7)
            dve.wait_ge(gates_out, 2 * JT)
            V.tensor_tensor(gate_i, gate_i, xc, ALU.mult).then_inc(ix_ok, 1)
            u_lo(8)
            dve.wait_ge(decay2_ok, 1)
            V.scalar_tensor_tensor(root, gate_r, 1.0, root, ALU.add, ALU.mult).then_inc(u_ok, 1)
            dve.wait_ge(u_ok, 1)
            V.tensor_scalar(root, root, 1e-34, None, ALU.max).then_inc(root2_ok, 1)
            u_lo(9)
            dve.wait_ge(root_ok, 1)
            dve.wait_ge(ix_ok, 1)
            V.tensor_tensor(gate_i, gate_i, root, ALU.mult).then_inc(u_ok, 1)
            dve.wait_ge(u_ok, 2)
            for j in range(JT):
                c = slice(j * SEQ, (j + 1) * SEQ)
                V.tensor_tensor_scan(xc[:, c], decay[:, c], gate_i[:, c], 0.0, ALU.mult, ALU.add).then_inc(scan_ok, 1)
            dve.wait_ge(scan_ok, JT)
            V.tensor_tensor(gelu, gelu, xc, ALU.mult).then_inc(lru_ok, 1)
            u_lo(10)
            u_lo(11)
            dve.wait_ge(lru_hi, 1)
            V.tensor_tensor(cat_lo[:, 4:8, :], gelu.rearrange("p (k c) -> p k c", k=4),
                            cat_hi[:, 4:8, :].bitcast(F32), ALU.subtract).then_inc(lru_lo, 1)

            def logits(h):
                dve.wait_ge(score_ok, h + 1)
                if h >= 2:
                    dve.wait_ge(pt_ok, h - 1)
                V.scalar_tensor_tensor(prob[:, h % 2, :], alibi[:], SLOPES[h], bank[4 + h % 2][:, 0:NB],
                                       ALU.mult, ALU.add).then_inc(logit_ok, 1)
                dve.wait_ge(logit_ok, h + 1)
                m = maxes[:, 2 * h:2 * h + 2]
                V.tensor_reduce(m[:, 0:1], prob[:, h % 2, 0:P], AX.X, ALU.max, negate=True).then_inc(max_half, 1)
                V.tensor_reduce(m[:, 1:2], prob[:, h % 2, P:NB], AX.X, ALU.max, negate=True).then_inc(max_ok, 1)

            def prob_out(h):
                dve.wait_ge(pt_ok, h + 1)
                if h >= 2:
                    dve.wait_ge(pv_ok, h - 1)
                V.tensor_copy(prob_t[:, h % 2, :], bank[7][:, 0:NB]).then_inc(pt_out, 1)

            def normalise(part):
                dve.wait_ge(prob_ok, 8 * (part + 1))
                V.reciprocal(rsums[:, part, :, :], sums[:, part, :, :]).then_inc(rsum_ok, 1)
                dve.wait_ge(rsum_ok, part + 1)
                dve.wait_ge(pv_ok, 4 * (part + 1))
                if part == 1:
                    dve.wait_ge(ot_ok, 1)
                V.tensor_tensor(o_nat[:, :, :].rearrange("p s (h d) -> p (s h) d", h=4),
                                bank[6][:, :].rearrange("p (a d) -> p a d", d=DH),
                                rsums[:, part, :, :].rearrange("p s h -> p (s h)").unsqueeze(2).to_broadcast([P, 2 * 4, DH]),
                                ALU.mult).then_inc(norm_ok, 1)

            def out_lo(part):
                b = bank[3] if part == 0 else bank[7]
                dve.wait_ge(ot_hi, part + 1)
                V.tensor_tensor(cat_lo[:, 2 * part:2 * part + 2, :], b[:, :].rearrange("p (k c) -> p k c", k=2),
                                cat_hi[:, 2 * part:2 * part + 2, :].bitcast(F32), ALU.subtract).then_inc(ot_lo, 1)

            dve.wait_ge(const_ok, 5)
            logits(0)
            logits(1)
            prob_out(0)
            logits(2)
            u_lo(12)
            prob_out(1)
            logits(3)
            prob_out(2)
            u_lo(13)
            prob_out(3)
            logits(4)
            logits(5)
            normalise(0)
            prob_out(4)
            logits(6)
            out_lo(0)
            prob_out(5)
            logits(7)
            prob_out(6)
            prob_out(7)
            normalise(1)
            out_lo(1)
            u_lo(14)

            def layer_norm(i, s, gain, shift, residual, done):
                for n in range(2):
                    residual(n)
                for n in range(2):
                    dve.wait_ge(res_ok, 2 * i + n + 1)
                    V.bn_stats(stats[:, s, n, :], xs[:, s, n * HALF:(n + 1) * HALF]).then_inc(ln_step, 1)
                dve.wait_ge(ln_step, 4 * i + 2)
                V.bn_aggr(mv[:, s, 0:2], stats[:, s, :, :].rearrange("p a b -> p (a b)")).then_inc(mv_ok, 1)
                for n in range(2):
                    c = slice(n * HALF, (n + 1) * HALF)
                    if n == 0:
                        dve.wait_ge(mv_ok, i + 1)
                    V.scalar_tensor_tensor(xs[:, s, c], xs[:, s, c], mv[:, s, 0:1], gain[:, c], ALU.subtract,
                                           ALU.mult).then_inc(ln_step, 1)
                    if n == 0:
                        dve.wait_ge(dev_ok, i + 1)
                        V.reciprocal(mv[:, s, 3:4], mv[:, s, 2:3]).then_inc(rdev_ok, 1)
                        dve.wait_ge(rdev_ok, i + 1)
                    dve.wait_ge(ln_step, 4 * i + 3 + n)
                    V.scalar_tensor_tensor(xs[:, s, c], xs[:, s, c], mv[:, s, 3:4], shift[:, c], ALU.mult,
                                           ALU.add).then_inc(done, 1)

            def ln1_of(s):
                def residual(n):
                    c = slice(n * HALF, (n + 1) * HALF)
                    dve.wait_ge(mix_ok, 2 * s + n + 1)
                    V.scalar_tensor_tensor(xs[:, s, c], xs[:, s, c], ALPHA, bank[2 * s + n][:, :], ALU.mult,
                                           ALU.add).then_inc(res_ok, 1)
                layer_norm(s, s, ln1[:, 0, :], ln1[:, 1, :], residual, x1_ok)

            dve.wait_ge(ln1_in, 2 * 16)
            ln1_of(0)
            x_lo(4, bank[6])
            x_lo(5, bank[7])
            u_lo(15)
            ln1_of(1)
            u_lo(16)
            x_lo(6, bank[0])
            x_lo(7, bank[1])
            u_lo(17)
            dve.wait_ge(ln2_in, 3 * 16)
            for s in range(ST):
                V.scalar_tensor_tensor(xs[:, s, :], xs[:, s, :], ALPHA, b_dn, ALU.mult, ALU.add).then_inc(res2_ok, 1)

            def hidden(g, par2, m):
                pair = 2 * g + m
                dve.wait_ge(relu_ok, 2 * pair + 2)
                V.tensor_tensor(sq_h[:, m, :], relu_h[:, m, :], relu_h[:, m, :], ALU.mult).then_inc(sq_ok, 1)
                dve.wait_ge(sq_ok, pair + 1)
                dve.wait_ge(hhi_ok, pair + 1)
                V.tensor_tensor(ht_lo[:, par2, 2 * m:2 * m + 2, :], sq_h[:, m, :].rearrange("p (k c) -> p k c", k=2),
                                ht_hi[:, par2, 2 * m:2 * m + 2, :].bitcast(F32), ALU.subtract).then_inc(hlo_ok, 1)

            def down_lo(g):
                for m in range(2):
                    unit_lo(unit_d(g) + m, 2 + m)

            hidden(0, 0, 0)
            hidden(0, 0, 1)
            down_lo(0)
            with dve.Fori(1, GROUPS - 1, 2) as g:
                for q in range(2):
                    for m in range(2):
                        hidden(g + q, 1 - q, m)
                        unit_lo(unit_u(g + q + 1) + m, m)
                    down_lo(g + q)
            hidden(GROUPS - 1, 1, 0)
            hidden(GROUPS - 1, 1, 1)
            for m in range(2):
                unit_lo(LAST_D + m, m)

            dve.wait_ge(res2_ok, ST)
            for s in range(ST):
                def residual(n, s=s):
                    c = slice(n * HALF, (n + 1) * HALF)
                    dve.wait_ge(y_ok, 2 * s + n + 1)
                    V.tensor_tensor(xs[:, s, c], xs[:, s, c], bank[2 * s + n][:, :], ALU.add).then_inc(res_ok, 1)
                layer_norm(2 + s, s, ln2[:, 0, :], ln2[:, 1, :], residual, out_ok)


_INS = ["x", "w_in", "conv_w", "conv_b", "w_rg", "b_rg", "w_ig", "b_ig", "lru_lambda", "w_out",
        "ln1_g", "ln1_b", "w_up", "b_up", "w_down", "b_down", "ln2_g", "ln2_b"]


def kernel(**inputs):
    import numpy as _np
    import concourse.bacc as _bacc
    from concourse import mybir as _mybir
    from concourse.bass_utils import run_bass_kernel_spmd as _run

    nc = _bacc.Bacc("TRN2", target_bir_lowering=False, num_devices=1)
    arrays, args = {}, []
    for name in _INS:
        a = _np.ascontiguousarray(inputs[name])
        arrays[f"in_{name}_dram"] = a
        args.append(nc.dram_tensor(f"in_{name}_dram", a.shape, _mybir.dt.from_np(a.dtype), kind="ExternalInput").ap())
    out = nc.dram_tensor("out_dram", inputs["x"].shape, _mybir.dt.float32, kind="ExternalOutput").ap()
    hybrid_layer(nc, *args, out)
    r = _run(nc, [arrays], core_ids=[0])
    return r.results[0]["out_dram"]
```

```python
from contextlib import ExitStack

import concourse.bass as bass
from concourse import mybir

F32 = mybir.dt.float32
F32R = mybir.dt.float32r
ACT = mybir.ActivationFunctionType
ALU = mybir.AluOpType
AX = mybir.AxisListType

P = 128
BANK = 512
RING = 4
UNIT = 2048
NEG = -1e30
WARM = 14
LN_EPS = 1e-5


def hybrid_layer(nc, x, w_in, conv_w, conv_b, w_rg, b_rg, w_ig, b_ig, lru_lambda, w_out,
                 ln1_g, ln1_b, w_up, b_up, w_down, b_down, ln2_g, ln2_b, out):
    _, SEQ, D = x.shape
    DEPTH = w_in.shape[0]
    ST = SEQ // P
    KT = D // P
    LRU_W = conv_w.shape[2]
    JT = LRU_W // P
    TAPS = conv_w.shape[1]
    ATT_W = D - LRU_W
    BLK = w_rg.shape[2]
    HEADS = 8
    DH = ATT_W // HEADS
    FF = w_up.shape[2]
    GROUPS = FF // 512
    FG = 4
    HALF = 512
    ALPHA = (2.0 * DEPTH) ** 0.25
    SCALE = DH ** -0.5
    SLOPES = [2.0 ** (-8.0 * (h + 1) / HEADS) for h in range(HEADS)]
    assert DEPTH == 1 and ST == 2 and KT == 8 and JT == 4 and ATT_W == 512 and GROUPS == 8 and TAPS == 4

    K0, V0, XR0, GR0 = ATT_W, 2 * ATT_W, 3 * ATT_W, 3 * ATT_W + LRU_W
    UNIT_COLS = [XR0, XR0 + 256, GR0, GR0 + 256, V0, V0 + 256, K0, 0, K0 + 256, 256]
    TILES = ([("xr", j) for j in range(4)] + [("gr", j) for j in range(4)]
             + [("v", j) for j in range(4)] + [("k", 0), ("k", 1), ("q", 0), ("q", 1)]
             + [("k", 2), ("k", 3), ("q", 2), ("q", 3)])
    N_IN = len(UNIT_COLS)
    N_OUT0 = N_IN
    N_UP0 = N_OUT0 + 4
    OUT_ROWS = [ATT_W, ATT_W + 256, 0, 256]

    def unit_u(g):
        return 4 * g + 12

    def unit_d(g):
        return 4 * g + 18

    LAST_D = 4 * (GROUPS - 1) + 16

    C_CW, C_CB, C_BR, C_BI, C_LAM, C_BUP = 0, 16, 20, 24, 28, 32
    N_PAR = C_BUP + FF // P

    with ExitStack() as ctx:
        def sb(name, shape, dt=F32):
            return ctx.enter_context(nc.sbuf_tensor(name, shape, dt))

        def sem(name):
            return ctx.enter_context(nc.semaphore(name))

        w_raw = sb("w_raw", [P, RING, UNIT])
        w_hi = sb("w_hi", [P, RING, UNIT], F32R)
        w_lo = sb("w_lo", [P, RING, UNIT], F32R)
        xs = sb("xs", [P, ST, D])
        xt_hi = sb("xt_hi", [P, KT, SEQ], F32R)
        xt_lo = sb("xt_lo", [P, KT, SEQ], F32R)
        cat_hi = sb("cat_hi", [P, KT, SEQ], F32R)
        cat_lo = sb("cat_lo", [P, KT, SEQ], F32R)
        ht_hi = sb("ht_hi", [P, 2, FG, SEQ], F32R)
        ht_lo = sb("ht_lo", [P, 2, FG, SEQ], F32R)
        u14_hi, u14_lo = (t[:, :, :, :].rearrange("p a f s -> p (a f s)").rearrange("p (k c) -> p k c", k=8)
                          for t in (ht_hi, ht_lo))
        ln1 = sb("ln1", [P, 2, D])
        XRP = SEQ + TAPS - 1
        area = sb("area", [P, JT * XRP + 5 * JT * SEQ])
        xrp = area[:, 0:JT * XRP].rearrange("p (j c) -> p j c", j=JT)

        def lru_part(n):
            a = JT * XRP + n * JT * SEQ
            return area[:, a:a + JT * SEQ]

        root = area[:, 0:JT * SEQ]
        xc, gate_r, gate_i, decay, gelu = (lru_part(n) for n in range(5))
        ln2 = area[:, 0:2 * D].rearrange("p (n d) -> p n d", n=2)
        b_dn = area[:, 2 * D:3 * D]
        relu_h = area[:, 3 * D:4 * D].rearrange("p (n d) -> p n d", n=2)
        sq_h = area[:, 4 * D:5 * D].rearrange("p (n d) -> p n d", n=2)
        qt = sb("qt", [P, JT, SEQ])
        kt = sb("kt", [P, JT, SEQ])
        vs = sb("vs", [P, ST, ATT_W])
        NB = 3 * P
        att = sb("att", [P, 4, NB])
        prob = att[:, 0:2, :]
        prob_t = att[:, 2:4, :]
        h_rows = att[:, :, :].rearrange("p a b -> p (a b)")[:, 0:2 * BANK].rearrange("p (n c) -> p n c", n=2)
        gate_w = att[:, :, :].rearrange("p a b -> p (a b)")[:, 0:2 * JT * P].rearrange(
            "p (g j c) -> p g j c", g=2, j=JT)
        o_nat = sb("o_nat", [P, ST, 256])
        alibi = sb("alibi", [P, NB])
        ident = sb("ident", [P, P])
        rows = sb("rows", [N_PAR, P])
        par = sb("par", [P, N_PAR])
        sp = sb("sp", [P, 10, 4])
        maxes = sb("maxes", [P, 2 * HEADS])
        sums = sb("sums", [P, 2, ST, 4])
        rsums = sb("rsums", [P, 2, ST, 4])
        stats = sb("stats", [P, ST, 2, 6])
        mv = sb("mv", [P, ST, 4])
        eps = sb("eps", [P, 1])

        bank = [ctx.enter_context(nc.psum_tensor(f"bank{n}", [P, BANK], F32)) for n in range(8)]

        x_in = [sem(f"x_in{n}") for n in range(2)]
        first_in = [sem(f"first_in{q}") for q in range(4)]
        first_hi, first_lo = sem("first_hi"), sem("first_lo")
        raw_in = [sem(f"raw_in{n}") for n in range(RING)]
        par_in, ln1_in, ln2_in, gw_in = sem("par_in"), sem("ln1_in"), sem("ln2_in"), sem("gw_in")
        out_done = sem("out_done")
        const_ok = sem("const_ok")
        pool_step = sem("pool_step")
        hi_ok, lo_ok = sem("hi_ok"), sem("lo_ok")
        par_t, par_ok, sp_z, sp_step, sp_ok = (sem("par_t"), sem("par_ok"), sem("sp_z"), sem("sp_step"),
                                               sem("sp_ok"))
        xt_t, xt_hi_ok, xt_lo_ok = sem("xt_t"), sem("xt_hi_ok"), sem("xt_lo_ok")
        proj_ok, proj_out = sem("proj_ok"), sem("proj_out")
        conv_step, conv_ok = sem("conv_step"), sem("conv_ok")
        gates_ok, gates_out = sem("gates_ok"), sem("gates_out")
        tanh_ok, decay_ok, decay2_ok = sem("tanh_ok"), sem("decay_ok"), sem("decay2_ok")
        root2_ok, root_ok, ix_ok, u_ok = sem("root2_ok"), sem("root_ok"), sem("ix_ok"), sem("u_ok")
        scan_ok, lru_ok, lru_hi, lru_lo = sem("scan_ok"), sem("lru_ok"), sem("lru_hi"), sem("lru_lo")
        score_ok, logit_ok, max_ok, prob_ok = sem("score_ok"), sem("logit_ok"), sem("max_ok"), sem("prob_ok")
        max_half = sem("max_half")
        pt_ok, pt_out, pv_ok = sem("pt_ok"), sem("pt_out"), sem("pv_ok")
        rsum_ok, norm_ok, ot_ok, ot_hi, ot_lo = (sem("rsum_ok"), sem("norm_ok"), sem("ot_ok"), sem("ot_hi"),
                                                 sem("ot_lo"))
        mix_ok, mix_part, res_ok, ln_step = sem("mix_ok"), sem("mix_part"), sem("res_ok"), sem("ln_step")
        mv_ok, dev_ok, rdev_ok, x1_ok = sem("mv_ok"), sem("dev_ok"), sem("rdev_ok"), sem("x1_ok")
        up_ok, relu_ok, sq_ok, hhi_ok, hlo_ok = (sem("up_ok"), sem("relu_ok"), sem("sq_ok"), sem("hhi_ok"),
                                                 sem("hlo_ok"))
        rows_ok, rows_out, turned = sem("rows_ok"), sem("rows_out"), sem("turned")
        down_ok, res2_ok, y_ok, out_ok = sem("down_ok"), sem("res2_ok"), sem("y_ok"), sem("out_ok")

        w_in_k = w_in[0].rearrange("(k p) c -> p k c", p=P)
        w_up_k = w_up[0].rearrange("(k p) c -> p k c", p=P)
        w_out_k = w_out[0].rearrange("(k p) c -> p k c", p=P)
        w_dn_k = w_down[0].rearrange("(k p) c -> p k c", p=P)

        def cols8(ring, slot):
            return ring[:, slot, :].rearrange("p (k c) -> p k c", k=8)

        def rows2(ring, slot):
            return ring[:, slot, :].rearrange("p (k c) -> p k c", k=2)

        block = ctx.enter_context(nc.Block())

        @block.sync
        def _(sp_e):
            def load_params():
                for c, v in ((C_CW, conv_w), (C_CB, conv_b), (C_BR, b_rg), (C_BI, b_ig), (C_LAM, lru_lambda),
                             (C_BUP, b_up)):
                    src = (v.rearrange("l t (j p) -> (l t j) p", p=P) if len(v.shape) == 3
                           else v.rearrange("l (j p) -> (l j) p", p=P))
                    sp_e.dma_start(rows[c:c + src.shape[0], :], src).then_inc(par_in, 16)

            for half in range(2):
                c = slice(half * HALF, (half + 1) * HALF)
                sp_e.dma_start(xs[:, :, c], x[0].rearrange("(s p) d -> p s d", p=P)[:, :, c]).then_inc(x_in[half], 16)
                for q in range(2 * half, 2 * half + 2):
                    k = slice(2 * q, 2 * q + 2)
                    sp_e.dma_start(cols8(w_raw, 0)[:, k, :],
                                   w_in_k[:, k, UNIT_COLS[0]:UNIT_COLS[0] + 256]).then_inc(first_in[q], 16)
            for n, c in enumerate(UNIT_COLS):
                if n == 0:
                    continue
                if n == 2:
                    load_params()
                if n >= RING:
                    sp_e.wait_ge(lo_ok, n - RING + 1)
                sp_e.dma_start(cols8(w_raw, n % RING), w_in_k[:, :, c:c + 256]).then_inc(raw_in[n % RING], 16)
            for m, r in enumerate(OUT_ROWS):
                n = N_OUT0 + m
                sp_e.wait_ge(lo_ok, n - RING + 1)
                sp_e.dma_start(rows2(w_raw, n % RING),
                               w_out_k[:, r // P:r // P + 2, :]).then_inc(raw_in[n % RING], 16)

            def load_up(g, n):
                for m in range(2):
                    slot = (2 if isinstance(g, int) and g == 0 else 0) + m
                    sp_e.wait_ge(lo_ok, n + m - RING + 1)
                    sp_e.dma_start(cols8(w_raw, slot),
                                   w_up_k[:, :, bass.ds(g * 512 + m * 256, 256)]).then_inc(raw_in[slot], 16)

            def load_down(g, n, slot=2):
                for m in range(2):
                    sp_e.wait_ge(lo_ok, n + m - RING + 1)
                    sp_e.dma_start(rows2(w_raw, slot + m),
                                   w_dn_k[:, bass.ds(g * 4 + 2 * m, 2), :]).then_inc(raw_in[slot + m], 16)

            load_up(0, N_UP0)
            load_up(1, N_UP0 + 2)
            load_down(0, unit_d(0))
            with sp_e.Fori(1, GROUPS - 1) as g:
                load_up(g + 1, unit_u(g + 1))
                load_down(g, unit_d(g))
            load_down(GROUPS - 1, LAST_D, 0)
            for s in range(ST):
                for n in range(2):
                    sp_e.wait_ge(out_ok, 2 * s + n + 1)
                    sp_e.dma_start(out[0, s * P:(s + 1) * P, n * HALF:(n + 1) * HALF],
                                   xs[:, s, n * HALF:(n + 1) * HALF]).then_inc(out_done, 16)
            sp_e.wait_ge(out_done, 16 * 2 * ST)

        @block.gpsimd
        def _(pool):
            nc.gpsimd.memset(ident[:], 0.0).then_inc(pool_step, 1)
            pool.wait_ge(pool_step, 1)
            nc.gpsimd.affine_select(out=ident[:], in_=ident[:], compare_op=ALU.not_equal, fill=1.0, base=0,
                                    pattern=[[-1, P]], channel_multiplier=1).then_inc(const_ok, 1)
            nc.gpsimd.memset(xrp[:, :, 0:TAPS - 1], 0.0).then_inc(const_ok, 1)
            nc.gpsimd.memset(eps[:], LN_EPS).then_inc(const_ok, 1)
            nc.gpsimd.memset(gate_w, 0.0).then_inc(pool_step, 1)
            pool.wait_ge(pool_step, 2)
            pool.wait_ge(lo_ok, 1)
            for n, w in enumerate((w_rg, w_ig)):
                blocks = w[0].rearrange("(j h) e f -> h e j f", h=2)
                for h in range(2):
                    pool.dma_start(gate_w[h * BLK:(h + 1) * BLK, n, :, h * BLK:(h + 1) * BLK],
                                   blocks[h]).then_inc(gw_in, 16)
            nc.gpsimd.iota(alibi[:, 0:P], [[1, P]], base=0, channel_multiplier=-1,
                           allow_small_or_imprecise_dtypes=True).then_inc(pool_step, 1)
            nc.gpsimd.iota(alibi[:, P:NB], [[1, 2 * P]], base=-P, channel_multiplier=-1,
                           allow_small_or_imprecise_dtypes=True).then_inc(pool_step, 1)
            pool.wait_ge(pool_step, 4)
            nc.gpsimd.affine_select(out=alibi[:, 0:P], in_=alibi[:, 0:P], compare_op=ALU.is_ge, fill=NEG,
                                    base=0, pattern=[[-1, P]], channel_multiplier=1).then_inc(const_ok, 1)
            nc.gpsimd.affine_select(out=alibi[:, P:NB], in_=alibi[:, P:NB], compare_op=ALU.is_ge, fill=NEG,
                                    base=P, pattern=[[-1, 2 * P]], channel_multiplier=1).then_inc(const_ok, 1)
            pool.wait_ge(lo_ok, 5)
            for n, v in enumerate((ln1_g, ln1_b)):
                pool.dma_start(ln1[:, n, :], v[0:1, :].to_broadcast([P, D])).then_inc(ln1_in, 16)
            pool.wait_ge(lru_lo, 1)
            for dst, v in ((ln2[:, 0, :], ln2_g), (ln2[:, 1, :], ln2_b), (b_dn, b_down)):
                pool.dma_start(dst, v[0:1, :].to_broadcast([P, D])).then_inc(ln2_in, 16)

        @block.tensor
        def _(pe):
            def mm3(dst, a_hi, a_lo, b_hi, b_lo, start, stop):
                pe.matmul(dst, a_hi, b_hi, start=start, stop=False)
                pe.matmul(dst, a_hi, b_lo, start=False, stop=False)
                return pe.matmul(dst, a_lo, b_hi, start=False, stop=stop)

            def transpose_x(s, half, to):
                for q in range(4):
                    c = (4 * half + q) * P
                    t = pe.transpose(to[:, q * P:(q + 1) * P], xs[:, s, c:c + P], ident[:])
                t.then_inc(xt_t, 1)

            pe.wait_ge(const_ok, 1)
            for n in range(WARM):
                pe.transpose(bank[0][:, 0:P], ident[:], ident[:])
            for half in range(2):
                pe.wait_ge(x_in[half], 16)
                for s in range(ST):
                    transpose_x(s, half, bank[4 + 2 * half + s])

            def first_unit():
                hi, lo = cols8(w_hi, 0), cols8(w_lo, 0)
                for q in range(4):
                    pe.wait_ge(xt_lo_ok, 2 + 2 * (q // 2))
                    if q < 3:
                        pe.wait_ge(first_lo, q + 1)
                    else:
                        pe.wait_ge(lo_ok, 1)
                    for n in range(2):
                        c = slice(n * P, (n + 1) * P)
                        for k in range(2 * q, 2 * q + 2):
                            i = mm3(bank[n][:, 0:256], hi[:, k, c], lo[:, k, c], xt_hi[:, k, :], xt_lo[:, k, :],
                                    k == 0, k == KT - 1)
                        if q == 3:
                            i.then_inc(proj_ok, 1)

            def proj(n):
                kind, j = TILES[n]
                u = n // 2
                slot = u % RING
                hi, lo = cols8(w_hi, slot), cols8(w_lo, slot)
                dst = bank[n % 3][:, 0:256]
                pe.wait_ge(lo_ok, u + 1)
                if n >= 3:
                    pe.wait_ge(proj_out, n - 2)
                for k in range(KT):
                    first, last = k == 0, k == KT - 1
                    if kind == "v":
                        s = slice((n % 2) * P, (n % 2 + 1) * P)
                        i = mm3(dst, xt_hi[:, k, s], xt_lo[:, k, s], hi[:, k, :], lo[:, k, :], first, last)
                    else:
                        c = slice((n % 2) * P, (n % 2 + 1) * P)
                        i = mm3(dst, hi[:, k, c], lo[:, k, c], xt_hi[:, k, :], xt_lo[:, k, :], first, last)
                i.then_inc(proj_ok, 1)

            def gates():
                pe.wait_ge(gw_in, 4 * 16)
                for j in range(JT):
                    pe.wait_ge(conv_ok, j + 1)
                    for n in range(2):
                        i = pe.matmul(bank[3 + j][:, n * SEQ:(n + 1) * SEQ], gate_w[:, n, j, :],
                                      xc[:, j * SEQ:(j + 1) * SEQ], start=True, stop=True)
                    i.then_inc(gates_ok, 1)

            def scores(h):
                b, j, r = bank[4 + h % 2], h // 2, slice(DH * (h % 2), DH * (h % 2) + DH)
                if h == 0:
                    pe.wait_ge(gates_out, 2 * JT)
                pe.wait_ge(proj_out, (15, 16, 19, 20)[j])
                if h >= 2:
                    pe.wait_ge(logit_ok, h - 1)
                pe.matmul(b[:, 0:P], qt[r, j, 0:P], kt[r, j, 0:P], start=True, stop=True)
                pe.matmul(b[:, P:NB], qt[r, j, P:SEQ], kt[r, j, :], start=True, stop=True).then_inc(score_ok, 1)

            def turn_prob(h):
                pe.wait_ge(prob_ok, 2 * (h + 1))
                if h >= 1:
                    pe.wait_ge(pt_out, h)
                for q in range(3):
                    t = pe.transpose(bank[7][:, q * P:(q + 1) * P], prob[:, h % 2, q * P:(q + 1) * P], ident[:])
                t.then_inc(pt_ok, 1)

            def values(h):
                pe.wait_ge(pt_out, h + 1)
                if h == 4:
                    pe.wait_ge(norm_ok, 1)
                v = slice(h * DH, (h + 1) * DH)
                c = (h % 4) * DH
                pt = prob_t[:, h % 2, :]
                pe.matmul(bank[6][:, c:c + DH], pt[:, 0:P], vs[:, 0, v], start=True, stop=True)
                pe.matmul(bank[6][:, 256 + c:256 + c + DH], pt[:, P:2 * P], vs[:, 0, v], start=True, stop=False)
                pe.matmul(bank[6][:, 256 + c:256 + c + DH], pt[:, 2 * P:NB], vs[:, 1, v],
                          start=False, stop=True).then_inc(pv_ok, 1)

            def turn_out(part):
                b = bank[3] if part == 0 else bank[7]
                pe.wait_ge(norm_ok, part + 1)
                if part == 1:
                    pe.wait_ge(pt_out, HEADS)
                for k in range(2):
                    for s in range(ST):
                        t = pe.transpose(b[:, k * SEQ + s * P:k * SEQ + (s + 1) * P],
                                         o_nat[:, s, k * P:(k + 1) * P], ident[:])
                t.then_inc(ot_ok, 1)

            def mix(s, n, part):
                units = {0: (10, 11), 1: (12,), 2: (13,)}[part]
                rows_at = {0: 4, 1: 0, 2: 2}[part]
                if part == 0:
                    pe.wait_ge(lru_lo, 1)
                    pe.wait_ge(proj_out, 20)
                    if s == 1 and n == 1:
                        pe.wait_ge(ot_lo, 1)
                else:
                    pe.wait_ge(ot_lo, part)
                for a, u in enumerate(units):
                    pe.wait_ge(lo_ok, u + 1)
                    for b in range(2):
                        k = rows_at + 2 * a + b
                        c = slice(n * HALF, (n + 1) * HALF)
                        i = mm3(bank[2 * s + n][:, :], cat_hi[:, k, s * P:(s + 1) * P],
                                cat_lo[:, k, s * P:(s + 1) * P], rows2(w_hi, u % RING)[:, b, c],
                                rows2(w_lo, u % RING)[:, b, c], k == 4, k == 3)
                if part == 2:
                    i.then_inc(mix_ok, 1)
                elif s == 1 and n == 1:
                    i.then_inc(mix_part, 1)

            first_unit()
            proj(2)
            pe.wait_ge(par_in, 6 * 16)
            pe.transpose(bank[3][:, 0:N_PAR], rows[:, :], ident[0:N_PAR, 0:N_PAR]).then_inc(par_t, 1)
            for n in range(3, 7):
                proj(n)
            gates()
            for n in range(7, 16):
                proj(n)
            pe.wait_ge(const_ok, 5)
            scores(0)
            scores(1)
            proj(16)
            turn_prob(0)
            scores(2)
            proj(17)
            values(0)
            turn_prob(1)
            scores(3)
            proj(18)
            values(1)
            turn_prob(2)
            proj(19)
            values(2)
            turn_prob(3)
            scores(4)
            scores(5)
            values(3)
            mix(0, 0, 0)
            turn_prob(4)
            scores(6)
            turn_prob(5)
            values(4)
            scores(7)
            mix(0, 1, 0)
            turn_prob(6)
            values(5)
            turn_out(0)
            turn_prob(7)
            values(6)
            mix(0, 0, 1)
            values(7)
            mix(0, 1, 1)
            turn_out(1)
            mix(1, 0, 0)
            mix(0, 0, 2)
            mix(0, 1, 2)
            mix(1, 1, 0)
            mix(1, 0, 1)
            mix(1, 1, 1)
            mix(1, 0, 2)
            for half in range(2):
                pe.wait_ge(x1_ok, half + 1)
                transpose_x(0, half, bank[6 + half])
            mix(1, 1, 2)

            def up(g, n, par2):
                for m in range(2):
                    hi, lo = cols8(w_hi, m), cols8(w_lo, m)
                    pe.wait_ge(lo_ok, n + m + 1)
                    pe.wait_ge(relu_ok, 4 * g - 6 + 2 * m)
                    for f in range(2):
                        for k in range(KT):
                            i = mm3(bank[4 + 2 * par2 + m][:, f * SEQ:(f + 1) * SEQ], hi[:, k, f * P:(f + 1) * P],
                                    lo[:, k, f * P:(f + 1) * P], xt_hi[:, k, :], xt_lo[:, k, :],
                                    k == 0, k == KT - 1)
                    i.then_inc(up_ok, 1)

            def up_rows(g, s):
                base, n0 = (2, N_UP0) if g == 0 else (0, N_UP0 + 2)
                for m in range(2):
                    hi, lo = (u14_hi, u14_lo) if n0 + m == N_UP0 else (cols8(w_hi, base + m), cols8(w_lo, base + m))
                    pe.wait_ge(lo_ok, n0 + m + 1)
                    for k in range(KT):
                        i = mm3(bank[2 * s + g][:, m * 256:(m + 1) * 256], xt_hi[:, k, s * P:(s + 1) * P],
                                xt_lo[:, k, s * P:(s + 1) * P], hi[:, k, :], lo[:, k, :], k == 0, k == KT - 1)
                    i.then_inc(rows_ok, 1)

            def turn_rows(nth, g, s):
                pe.wait_ge(rows_out, nth + 1)
                for f in range(FG):
                    b = bank[4 + 2 * g + f // 2]
                    a = (f % 2) * SEQ + s * P
                    i = pe.transpose(b[:, a:a + P], h_rows[:, nth % 2, f * P:(f + 1) * P], ident[:])
                    if s == 1 and f % 2 == 1:
                        i.then_inc(up_ok, 1)
                    elif f == FG - 1:
                        i.then_inc(turned, 1)

            def down(g, par2, first=False, last=False):
                slot = 0 if last else 2
                pe.wait_ge(hlo_ok, 2 * g + 2)
                for s in range(ST):
                    if first and s == 1:
                        turn_rows(3, 1, 1)
                    for n in range(2):
                        c = slice(n * HALF, (n + 1) * HALF)
                        for f in range(FG):
                            if s == 0 and n == 0 and f % 2 == 0:
                                pe.wait_ge(lo_ok, (LAST_D if last else unit_d(g)) + f // 2 + 1)
                            i = mm3(bank[2 * s + n][:, :], ht_hi[:, par2, f, s * P:(s + 1) * P],
                                    ht_lo[:, par2, f, s * P:(s + 1) * P], rows2(w_hi, slot + f // 2)[:, f % 2, c],
                                    rows2(w_lo, slot + f // 2)[:, f % 2, c], first and f == 0, last and f == FG - 1)
                        if last:
                            i.then_inc(y_ok, 1)
                if not last:
                    i.then_inc(down_ok, 1)

            pe.wait_ge(xt_lo_ok, 6)
            up_rows(0, 0)
            up_rows(1, 0)
            for half in range(2):
                pe.wait_ge(x1_ok, 2 + half + 1)
                transpose_x(1, half, bank[4 + half])
            pe.wait_ge(xt_lo_ok, 8)
            turn_rows(0, 0, 0)
            up_rows(0, 1)
            turn_rows(1, 1, 0)
            turn_rows(2, 0, 1)
            up_rows(1, 1)
            pe.wait_ge(rows_out, 3)
            down(0, 0, first=True)
            with pe.Fori(1, GROUPS - 1, 2) as g:
                for q in range(2):
                    up(g + q + 1, unit_u(g + q + 1), q)
                    down(g + q, 1 - q)
            down(GROUPS - 1, 1, last=True)

        @block.scalar
        def _(act):
            A = nc.scalar.activation
            def x_hi(n, s, half, src):
                act.wait_ge(xt_t, n + 1)
                nc.scalar.copy(xt_hi[:, 4 * half:4 * half + 4, s * P:(s + 1) * P],
                               src[:, :].rearrange("p (k c) -> p k c", k=4)).then_inc(xt_hi_ok, 1)

            def unit_hi(slot, nth, user, uses):
                if isinstance(slot, int) and slot == 0:
                    nth = nth - 1
                act.wait_ge(raw_in[slot], 16 * nth)
                if user is not None:
                    act.wait_ge(user, uses)
                nc.scalar.copy(w_hi[:, slot, :], w_raw[:, slot, :]).then_inc(hi_ok, 1)

            def first_hi_part(q):
                k = slice(2 * q, 2 * q + 2)
                act.wait_ge(first_in[q], 16)
                nc.scalar.copy(cols8(w_hi, 0)[:, k, :], cols8(w_raw, 0)[:, k, :]).then_inc(
                    first_hi if q < 3 else hi_ok, 1)

            def u_hi(n):
                if n < RING:
                    user, uses = None, 0
                elif n < RING + N_IN:
                    user, uses = proj_ok, 2 * (n - RING + 1)
                else:
                    user, uses = ((mix_part, 1), (mix_part, 2), (mix_ok, 4))[n - N_UP0 - 1]
                unit_hi(n % RING, n // RING + 1, user, uses)

            def proj_evict(n):
                kind, j = TILES[n]
                src = bank[n % 3][:, 0:256]
                act.wait_ge(proj_ok, n + 1)
                if kind == "xr":
                    i = nc.scalar.copy(xrp[:, j, TAPS - 1:], src)
                elif kind == "gr":
                    i = A(gelu[:, j * SEQ:(j + 1) * SEQ], src, ACT.Gelu_apprx_tanh)
                elif kind == "v":
                    i = nc.scalar.copy(vs[:, j % 2, (j // 2) * 256:(j // 2 + 1) * 256], src)
                elif kind == "k":
                    i = nc.scalar.copy(kt[:, j, :], src)
                else:
                    i = nc.scalar.mul(qt[:, j, :], src, SCALE)
                i.then_inc(proj_out, 1)

            def exps(h):
                act.wait_ge(max_ok, h + 1)
                for s, c in ((0, slice(0, P)), (1, slice(P, NB))):
                    A(prob[:, h % 2, c], prob[:, h % 2, c], ACT.Exp, bias=maxes[:, 2 * h + s:2 * h + s + 1],
                      accum_out=sums[:, h // 4, s, h % 4:h % 4 + 1]).then_inc(prob_ok, 1)

            def out_hi(part):
                b = bank[3] if part == 0 else bank[7]
                act.wait_ge(ot_ok, part + 1)
                nc.scalar.copy(cat_hi[:, 2 * part:2 * part + 2, :],
                               b[:, :].rearrange("p (k c) -> p k c", k=2)).then_inc(ot_hi, 1)

            for half in range(2):
                for s in range(ST):
                    x_hi(2 * half + s, s, half, bank[4 + 2 * half + s])
                first_hi_part(2 * half)
                first_hi_part(2 * half + 1)
            u_hi(1)
            u_hi(2)
            act.wait_ge(const_ok, 2)
            proj_evict(0)
            u_hi(3)
            proj_evict(1)
            u_hi(4)
            act.wait_ge(sp_step, 2)
            A(sp[:, 1, :], sp[:, 0, :], ACT.Exp, scale=-1.0).then_inc(sp_z, 1)
            for n in range(2, 8):
                proj_evict(n)
                if n % 2:
                    u_hi(n // 2 + 4)
            for j in range(JT):
                act.wait_ge(gates_ok, j + 1)
                for n, (dst, c) in enumerate(((gate_r, C_BR), (gate_i, C_BI))):
                    A(dst[:, j * SEQ:(j + 1) * SEQ], bank[3 + j][:, n * SEQ:(n + 1) * SEQ], ACT.Sigmoid,
                      bias=par[:, c + j:c + j + 1]).then_inc(gates_out, 1)
            proj_evict(8)
            proj_evict(9)
            u_hi(8)
            act.wait_ge(sp_ok, 2)
            act.wait_ge(gates_out, 2 * JT)
            act.wait_ge(conv_ok, JT)
            for j in range(JT):
                c = slice(j * SEQ, (j + 1) * SEQ)
                A(root[:, c], gate_r[:, c], ACT.Tanh, scale=sp[:, 8, j:j + 1]).then_inc(tanh_ok, 1)
            for j in range(JT):
                c = slice(j * SEQ, (j + 1) * SEQ)
                A(decay[:, c], gate_r[:, c], ACT.Exp, scale=sp[:, 9, j:j + 1]).then_inc(decay_ok, 1)
            proj_evict(10)
            act.wait_ge(decay_ok, JT)
            act.wait_ge(tanh_ok, JT)
            A(gate_r, decay, ACT.Square).then_inc(decay2_ok, 1)
            proj_evict(11)
            u_hi(9)
            act.wait_ge(root2_ok, 1)
            A(root, root, ACT.Sqrt).then_inc(root_ok, 1)
            proj_evict(12)
            proj_evict(13)
            proj_evict(14)
            proj_evict(15)
            exps(0)
            exps(1)
            act.wait_ge(lru_ok, 1)
            nc.scalar.copy(cat_hi[:, 4:8, :], gelu.rearrange("p (k c) -> p k c", k=4)).then_inc(lru_hi, 1)
            proj_evict(16)
            u_hi(10)
            exps(2)
            proj_evict(17)
            u_hi(11)
            exps(3)
            proj_evict(18)
            u_hi(12)
            proj_evict(19)
            u_hi(13)
            exps(4)
            exps(5)
            exps(6)
            exps(7)
            out_hi(0)
            act.wait_ge(raw_in[2], 16 * 4)
            nc.scalar.copy(u14_hi, cols8(w_raw, 2)).then_inc(hi_ok, 1)
            out_hi(1)

            def deviation(i, s):
                act.wait_ge(mv_ok, i + 1)
                A(mv[:, s, 2:3], mv[:, s, 1:2], ACT.Sqrt, bias=eps[:]).then_inc(dev_ok, 1)

            deviation(0, 0)
            u_hi(15)
            x_hi(4, 0, 0, bank[6])
            x_hi(5, 0, 1, bank[7])
            u_hi(16)
            u_hi(17)
            act.wait_ge(ln2_in, 3 * 16)

            def rows_evict(nth, g, s):
                act.wait_ge(rows_ok, 2 * nth + 2)
                if nth == 2:
                    act.wait_ge(turned, 1)
                elif nth == 3:
                    act.wait_ge(turned, 2)
                nc.scalar.copy(h_rows[:, nth % 2, :], bank[2 * s + g][:, :]).then_inc(rows_out, 1)

            rows_evict(0, 0, 0)
            deviation(1, 1)
            rows_evict(1, 1, 0)
            x_hi(6, 1, 0, bank[4])
            x_hi(7, 1, 1, bank[5])
            unit_hi(2, 5, mix_part, 1)
            rows_evict(2, 0, 1)
            unit_hi(3, 5, rows_ok, 6)

            def hidden(g, par2, m):
                pe_pair = 2 * g + m
                act.wait_ge(up_ok, pe_pair + 1)
                if not (isinstance(g, int) and g == 0):
                    act.wait_ge(hlo_ok, pe_pair - 1)
                for f in range(2):
                    A(relu_h[:, m, f * SEQ:(f + 1) * SEQ], bank[4 + 2 * par2 + m][:, f * SEQ:(f + 1) * SEQ],
                      ACT.Relu, bias=par[:, bass.ds(C_BUP + 4 * g + 2 * m + f, 1)]).then_inc(relu_ok, 1)
                act.wait_ge(relu_ok, 2 * pe_pair + 2)
                A(ht_hi[:, par2, 2 * m:2 * m + 2, :], relu_h[:, m, :].rearrange("p (k c) -> p k c", k=2),
                  ACT.Square).then_inc(hhi_ok, 1)

            def down_hi(g):
                for m in range(2):
                    unit_hi(2 + m, g + 5, down_ok, g)

            hidden(0, 0, 0)
            hidden(0, 0, 1)
            rows_evict(3, 1, 1)
            with act.Fori(1, GROUPS - 1, 2) as g:
                for q in range(2):
                    for m in range(2):
                        hidden(g + q, 1 - q, m)
                        unit_hi(m, g + q + 5, up_ok, 2 * (g + q) + m + 1)
                    down_hi(g + q)
            hidden(GROUPS - 1, 1, 0)
            hidden(GROUPS - 1, 1, 1)
            for m in range(2):
                unit_hi(m, GROUPS + 4, up_ok, 2 * (GROUPS - 1) + m + 1)
            deviation(2, 0)
            deviation(3, 1)

        @block.vector
        def _(dve):
            V = nc.vector

            def x_lo(n, s, half, src):
                dst = (slice(None), slice(4 * half, 4 * half + 4), slice(s * P, (s + 1) * P))
                dve.wait_ge(xt_hi_ok, n + 1)
                V.tensor_tensor(xt_lo[dst], src[:, :].rearrange("p (k c) -> p k c", k=4),
                                xt_hi[dst].bitcast(F32), ALU.subtract).then_inc(xt_lo_ok, 1)

            def unit_lo(n, slot):
                dve.wait_ge(hi_ok, n + 1)
                V.tensor_tensor(w_lo[:, slot, :], w_raw[:, slot, :], w_hi[:, slot, :].bitcast(F32),
                                ALU.subtract).then_inc(lo_ok, 1)

            def u_lo(n):
                unit_lo(n, n % RING)

            steps = [0]

            def step(i):
                steps[0] += 1
                i.then_inc(sp_step, 1)
                dve.wait_ge(sp_step, steps[0])

            def first_lo_part(q):
                k = slice(2 * q, 2 * q + 2)
                if q < 3:
                    dve.wait_ge(first_hi, q + 1)
                else:
                    dve.wait_ge(hi_ok, 1)
                V.tensor_tensor(cols8(w_lo, 0)[:, k, :], cols8(w_raw, 0)[:, k, :],
                                cols8(w_hi, 0)[:, k, :].bitcast(F32), ALU.subtract).then_inc(
                    first_lo if q < 3 else lo_ok, 1)

            for half in range(2):
                for s in range(ST):
                    x_lo(2 * half + s, s, half, bank[4 + 2 * half + s])
                first_lo_part(2 * half)
                first_lo_part(2 * half + 1)
            u_lo(1)
            u_lo(2)
            dve.wait_ge(par_t, 1)
            V.tensor_copy(par[:], bank[3][:, 0:N_PAR]).then_inc(par_ok, 1)
            dve.wait_ge(par_ok, 1)
            lam = par[:, C_LAM:C_LAM + 4]
            step(V.tensor_scalar(sp[:, 2, :], lam, -1.0, None, ALU.mult))
            step(V.tensor_tensor(sp[:, 0, :], lam, sp[:, 2, :], ALU.max))

            def conv(j):
                dst = xc[:, j * SEQ:(j + 1) * SEQ]
                dve.wait_ge(proj_out, j + 1)
                V.tensor_scalar(dst, xrp[:, j, 0:SEQ], par[:, C_CW + j:C_CW + j + 1],
                                par[:, C_CB + j:C_CB + j + 1], ALU.mult, ALU.add).then_inc(conv_step, 1)
                for t in range(1, TAPS):
                    dve.wait_ge(conv_step, 3 * j + t)
                    c = C_CW + JT * t + j
                    V.scalar_tensor_tensor(dst, xrp[:, j, t:t + SEQ], par[:, c:c + 1], dst, ALU.mult,
                                           ALU.add).then_inc(conv_ok if t == TAPS - 1 else conv_step, 1)

            dve.wait_ge(const_ok, 2)
            conv(0)
            u_lo(3)
            conv(1)
            u_lo(4)
            conv(2)
            conv(3)
            u_lo(5)
            u_lo(6)
            u_lo(7)

            dve.wait_ge(sp_z, 1)
            step(V.tensor_scalar(sp[:, 3, :], sp[:, 1, :], 2.0, None, ALU.add))
            step(V.reciprocal(sp[:, 4, :], sp[:, 3, :]))
            step(V.tensor_tensor(sp[:, 5, :], sp[:, 1, :], sp[:, 4, :], ALU.mult))
            step(V.tensor_tensor(sp[:, 6, :], sp[:, 5, :], sp[:, 5, :], ALU.mult))
            step(V.tensor_scalar(sp[:, 7, :], sp[:, 6, :], 1.0 / 15, None, ALU.mult))
            for c in (13, 11, 9, 7, 5, 3):
                step(V.scalar_tensor_tensor(sp[:, 7, :], sp[:, 7, :], 1.0 / c, sp[:, 6, :], ALU.add, ALU.mult))
            step(V.scalar_tensor_tensor(sp[:, 7, :], sp[:, 7, :], 1.0, sp[:, 5, :], ALU.add, ALU.mult))
            step(V.tensor_scalar(sp[:, 2, :], sp[:, 2, :], 0.0, 8.0, ALU.max, ALU.mult))
            V.scalar_tensor_tensor(sp[:, 8, :], sp[:, 7, :], 16.0, sp[:, 2, :], ALU.mult, ALU.add).then_inc(sp_ok, 1)
            dve.wait_ge(sp_ok, 1)
            V.tensor_scalar(sp[:, 9, :], sp[:, 8, :], -1.0, None, ALU.mult).then_inc(sp_ok, 1)

            dve.wait_ge(gates_out, 2 * JT)
            V.tensor_tensor(gate_i, gate_i, xc, ALU.mult).then_inc(ix_ok, 1)
            u_lo(8)
            dve.wait_ge(decay2_ok, 1)
            V.scalar_tensor_tensor(root, gate_r, 1.0, root, ALU.add, ALU.mult).then_inc(u_ok, 1)
            dve.wait_ge(u_ok, 1)
            V.tensor_scalar(root, root, 1e-34, None, ALU.max).then_inc(root2_ok, 1)
            u_lo(9)
            dve.wait_ge(root_ok, 1)
            dve.wait_ge(ix_ok, 1)
            V.tensor_tensor(gate_i, gate_i, root, ALU.mult).then_inc(u_ok, 1)
            dve.wait_ge(u_ok, 2)
            for j in range(JT):
                c = slice(j * SEQ, (j + 1) * SEQ)
                V.tensor_tensor_scan(xc[:, c], decay[:, c], gate_i[:, c], 0.0, ALU.mult, ALU.add).then_inc(scan_ok, 1)
            dve.wait_ge(scan_ok, JT)
            V.tensor_tensor(gelu, gelu, xc, ALU.mult).then_inc(lru_ok, 1)
            def lru_split():
                dve.wait_ge(lru_hi, 1)
                V.tensor_tensor(cat_lo[:, 4:8, :], gelu.rearrange("p (k c) -> p k c", k=4),
                                cat_hi[:, 4:8, :].bitcast(F32), ALU.subtract).then_inc(lru_lo, 1)

            def logits(h):
                dve.wait_ge(score_ok, h + 1)
                if h >= 2:
                    dve.wait_ge(pt_ok, h - 1)
                V.scalar_tensor_tensor(prob[:, h % 2, :], alibi[:], SLOPES[h], bank[4 + h % 2][:, 0:NB],
                                       ALU.mult, ALU.add).then_inc(logit_ok, 1)
                dve.wait_ge(logit_ok, h + 1)
                m = maxes[:, 2 * h:2 * h + 2]
                V.tensor_reduce(m[:, 0:1], prob[:, h % 2, 0:P], AX.X, ALU.max, negate=True).then_inc(max_half, 1)
                V.tensor_reduce(m[:, 1:2], prob[:, h % 2, P:NB], AX.X, ALU.max, negate=True).then_inc(max_ok, 1)

            def prob_out(h):
                dve.wait_ge(pt_ok, h + 1)
                if h >= 2:
                    dve.wait_ge(pv_ok, h - 1)
                V.tensor_copy(prob_t[:, h % 2, :], bank[7][:, 0:NB]).then_inc(pt_out, 1)

            def normalise(part):
                dve.wait_ge(prob_ok, 8 * (part + 1))
                V.reciprocal(rsums[:, part, :, :], sums[:, part, :, :]).then_inc(rsum_ok, 1)
                dve.wait_ge(rsum_ok, part + 1)
                dve.wait_ge(pv_ok, 4 * (part + 1))
                if part == 1:
                    dve.wait_ge(ot_ok, 1)
                V.tensor_tensor(o_nat[:, :, :].rearrange("p s (h d) -> p (s h) d", h=4),
                                bank[6][:, :].rearrange("p (a d) -> p a d", d=DH),
                                rsums[:, part, :, :].rearrange("p s h -> p (s h)").unsqueeze(2).to_broadcast([P, 2 * 4, DH]),
                                ALU.mult).then_inc(norm_ok, 1)

            def out_lo(part):
                b = bank[3] if part == 0 else bank[7]
                dve.wait_ge(ot_hi, part + 1)
                V.tensor_tensor(cat_lo[:, 2 * part:2 * part + 2, :], b[:, :].rearrange("p (k c) -> p k c", k=2),
                                cat_hi[:, 2 * part:2 * part + 2, :].bitcast(F32), ALU.subtract).then_inc(ot_lo, 1)

            dve.wait_ge(const_ok, 5)
            logits(0)
            logits(1)
            prob_out(0)
            lru_split()
            logits(2)
            u_lo(10)
            prob_out(1)
            logits(3)
            u_lo(11)
            prob_out(2)
            u_lo(12)
            prob_out(3)
            logits(4)
            logits(5)
            normalise(0)
            prob_out(4)
            logits(6)
            prob_out(5)
            logits(7)
            u_lo(13)
            prob_out(6)
            out_lo(0)
            prob_out(7)
            normalise(1)
            dve.wait_ge(hi_ok, N_UP0 + 1)
            V.tensor_tensor(u14_lo, cols8(w_raw, 2), u14_hi.bitcast(F32), ALU.subtract).then_inc(lo_ok, 1)
            out_lo(1)

            def layer_norm(i, s, gain, shift, residual, done):
                for n in range(2):
                    residual(n)
                    dve.wait_ge(res_ok, 2 * i + n + 1)
                    V.bn_stats(stats[:, s, n, :], xs[:, s, n * HALF:(n + 1) * HALF]).then_inc(ln_step, 1)
                dve.wait_ge(ln_step, 4 * i + 2)
                V.bn_aggr(mv[:, s, 0:2], stats[:, s, :, :].rearrange("p a b -> p (a b)")).then_inc(mv_ok, 1)
                for n in range(2):
                    c = slice(n * HALF, (n + 1) * HALF)
                    if n == 0:
                        dve.wait_ge(mv_ok, i + 1)
                    V.scalar_tensor_tensor(xs[:, s, c], xs[:, s, c], mv[:, s, 0:1], gain[:, c], ALU.subtract,
                                           ALU.mult).then_inc(ln_step, 1)
                    if n == 0:
                        dve.wait_ge(dev_ok, i + 1)
                        V.reciprocal(mv[:, s, 3:4], mv[:, s, 2:3]).then_inc(rdev_ok, 1)
                        dve.wait_ge(rdev_ok, i + 1)
                    dve.wait_ge(ln_step, 4 * i + 3 + n)
                    V.scalar_tensor_tensor(xs[:, s, c], xs[:, s, c], mv[:, s, 3:4], shift[:, c], ALU.mult,
                                           ALU.add).then_inc(done, 1)

            def ln1_of(s):
                def residual(n):
                    c = slice(n * HALF, (n + 1) * HALF)
                    dve.wait_ge(mix_ok, 2 * s + n + 1)
                    V.scalar_tensor_tensor(xs[:, s, c], xs[:, s, c], ALPHA, bank[2 * s + n][:, :], ALU.mult,
                                           ALU.add).then_inc(res_ok, 1)
                layer_norm(s, s, ln1[:, 0, :], ln1[:, 1, :], residual, x1_ok)

            dve.wait_ge(ln1_in, 2 * 16)
            ln1_of(0)
            x_lo(4, 0, 0, bank[6])
            x_lo(5, 0, 1, bank[7])
            u_lo(15)
            u_lo(16)
            u_lo(17)
            ln1_of(1)
            x_lo(6, 1, 0, bank[4])
            x_lo(7, 1, 1, bank[5])
            unit_lo(unit_d(0), 2)
            dve.wait_ge(ln2_in, 3 * 16)
            for s in range(ST):
                V.scalar_tensor_tensor(xs[:, s, :], xs[:, s, :], ALPHA, b_dn, ALU.mult, ALU.add).then_inc(res2_ok, 1)

            def hidden(g, par2, m):
                pair = 2 * g + m
                dve.wait_ge(relu_ok, 2 * pair + 2)
                V.tensor_tensor(sq_h[:, m, :], relu_h[:, m, :], relu_h[:, m, :], ALU.mult).then_inc(sq_ok, 1)
                dve.wait_ge(sq_ok, pair + 1)
                dve.wait_ge(hhi_ok, pair + 1)
                V.tensor_tensor(ht_lo[:, par2, 2 * m:2 * m + 2, :], sq_h[:, m, :].rearrange("p (k c) -> p k c", k=2),
                                ht_hi[:, par2, 2 * m:2 * m + 2, :].bitcast(F32), ALU.subtract).then_inc(hlo_ok, 1)

            def down_lo(g):
                for m in range(2):
                    unit_lo(unit_d(g) + m, 2 + m)

            unit_lo(unit_d(0) + 1, 3)
            hidden(0, 0, 0)
            hidden(0, 0, 1)
            with dve.Fori(1, GROUPS - 1, 2) as g:
                for q in range(2):
                    for m in range(2):
                        hidden(g + q, 1 - q, m)
                        unit_lo(unit_u(g + q + 1) + m, m)
                    down_lo(g + q)
            hidden(GROUPS - 1, 1, 0)
            hidden(GROUPS - 1, 1, 1)
            for m in range(2):
                unit_lo(LAST_D + m, m)

            dve.wait_ge(res2_ok, ST)
            for s in range(ST):
                def residual(n, s=s):
                    c = slice(n * HALF, (n + 1) * HALF)
                    dve.wait_ge(y_ok, 2 * s + n + 1)
                    V.tensor_tensor(xs[:, s, c], xs[:, s, c], bank[2 * s + n][:, :], ALU.add).then_inc(res_ok, 1)
                layer_norm(2 + s, s, ln2[:, 0, :], ln2[:, 1, :], residual, out_ok)


_INS = ["x", "w_in", "conv_w", "conv_b", "w_rg", "b_rg", "w_ig", "b_ig", "lru_lambda", "w_out",
        "ln1_g", "ln1_b", "w_up", "b_up", "w_down", "b_down", "ln2_g", "ln2_b"]


def kernel(**inputs):
    import numpy as _np
    import concourse.bacc as _bacc
    from concourse import mybir as _mybir
    from concourse.bass_utils import run_bass_kernel_spmd as _run

    nc = _bacc.Bacc("TRN2", target_bir_lowering=False, num_devices=1)
    arrays, args = {}, []
    for name in _INS:
        a = _np.ascontiguousarray(inputs[name])
        arrays[f"in_{name}_dram"] = a
        args.append(nc.dram_tensor(f"in_{name}_dram", a.shape, _mybir.dt.from_np(a.dtype), kind="ExternalInput").ap())
    out = nc.dram_tensor("out_dram", inputs["x"].shape, _mybir.dt.float32, kind="ExternalOutput").ap()
    hybrid_layer(nc, *args, out)
    r = _run(nc, [arrays], core_ids=[0])
    return r.results[0]["out_dram"]
```

```python
from contextlib import ExitStack

import concourse.bass as bass
from concourse import mybir

F32 = mybir.dt.float32
F32R = mybir.dt.float32r
ACT = mybir.ActivationFunctionType
ALU = mybir.AluOpType
AX = mybir.AxisListType

P = 128
BANK = 512
RING = 4
UNIT = 2048
FIRST = 3
NEG = -1e30
WARM, WARM_MORE = 10, 6
LN_EPS = 1e-5


def hybrid_layer(nc, x, w_in, conv_w, conv_b, w_rg, b_rg, w_ig, b_ig, lru_lambda, w_out,
                 ln1_g, ln1_b, w_up, b_up, w_down, b_down, ln2_g, ln2_b, out):
    _, SEQ, D = x.shape
    DEPTH = w_in.shape[0]
    ST = SEQ // P
    KT = D // P
    LRU_W = conv_w.shape[2]
    JT = LRU_W // P
    TAPS = conv_w.shape[1]
    ATT_W = D - LRU_W
    BLK = w_rg.shape[2]
    HEADS = 8
    DH = ATT_W // HEADS
    FF = w_up.shape[2]
    GROUPS = FF // 512
    FG = 4
    HALF = 512
    ALPHA = (2.0 * DEPTH) ** 0.25
    SCALE = DH ** -0.5
    SLOPES = [2.0 ** (-8.0 * (h + 1) / HEADS) for h in range(HEADS)]
    assert DEPTH == 1 and ST == 2 and KT == 8 and JT == 4 and ATT_W == 512 and GROUPS == 8 and TAPS == 4

    K0, V0, XR0, GR0 = ATT_W, 2 * ATT_W, 3 * ATT_W, 3 * ATT_W + LRU_W
    UNIT_COLS = [XR0, XR0 + 256, GR0, GR0 + 256, V0, V0 + 256, K0, 0, K0 + 256, 256]
    TILES = ([("xr", j) for j in range(4)] + [("gr", j) for j in range(4)]
             + [("v", j) for j in range(4)] + [("k", 0), ("k", 1), ("q", 0), ("q", 1)]
             + [("k", 2), ("k", 3), ("q", 2), ("q", 3)])
    N_IN = len(UNIT_COLS)
    N_OUT0 = N_IN
    N_UP0 = N_OUT0 + 4
    OUT_ROWS = [ATT_W, ATT_W + 256, 0, 256]

    def unit_u(g):
        return 4 * g + 12

    def unit_d(g):
        return 4 * g + 18

    LAST_D = 4 * (GROUPS - 1) + 16

    C_CW, C_CB, C_BR, C_BI, C_LAM, C_BUP = 0, 16, 20, 24, 28, 32
    N_PAR = C_BUP + FF // P

    with ExitStack() as ctx:
        def sb(name, shape, dt=F32):
            return ctx.enter_context(nc.sbuf_tensor(name, shape, dt))

        def sem(name):
            return ctx.enter_context(nc.semaphore(name))

        w_raw = sb("w_raw", [P, RING, UNIT])
        w_hi = sb("w_hi", [P, RING, UNIT], F32R)
        w_lo = sb("w_lo", [P, RING, UNIT], F32R)
        xs = sb("xs", [P, ST, D])
        xt_hi = sb("xt_hi", [P, KT, SEQ], F32R)
        xt_lo = sb("xt_lo", [P, KT, SEQ], F32R)
        cat_hi = sb("cat_hi", [P, KT, SEQ], F32R)
        cat_lo = sb("cat_lo", [P, KT, SEQ], F32R)
        ht_hi = sb("ht_hi", [P, 2, FG, SEQ], F32R)
        ht_lo = sb("ht_lo", [P, 2, FG, SEQ], F32R)
        u14_hi, u14_lo = (t[:, :, :, :].rearrange("p a f s -> p (a f s)").rearrange("p (k c) -> p k c", k=8)
                          for t in (ht_hi, ht_lo))
        ln1 = sb("ln1", [P, 2, D])
        XRP = SEQ + TAPS - 1
        area = sb("area", [P, JT * XRP + 5 * JT * SEQ])
        xrp = area[:, 0:JT * XRP].rearrange("p (j c) -> p j c", j=JT)

        def lru_part(n):
            a = JT * XRP + n * JT * SEQ
            return area[:, a:a + JT * SEQ]

        root = area[:, 0:JT * SEQ]
        xc, gate_r, gate_i, decay, gelu = (lru_part(n) for n in range(5))
        ln2 = area[:, 0:2 * D].rearrange("p (n d) -> p n d", n=2)
        b_dn = area[:, 2 * D:3 * D]
        relu_h = area[:, 3 * D:4 * D].rearrange("p (n d) -> p n d", n=2)
        sq_h = area[:, 4 * D:5 * D].rearrange("p (n d) -> p n d", n=2)
        qt = sb("qt", [P, JT, SEQ])
        kt = sb("kt", [P, JT, SEQ])
        vs = sb("vs", [P, ST, ATT_W])
        NB = 3 * P
        att = sb("att", [P, 4, NB])
        prob = att[:, 0:2, :]
        prob_t = att[:, 2:4, :]
        h_rows = att[:, :, :].rearrange("p a b -> p (a b)")[:, 0:2 * BANK].rearrange("p (n c) -> p n c", n=2)
        gate_w = att[:, :, :].rearrange("p a b -> p (a b)")[:, 0:2 * JT * P].rearrange(
            "p (g j c) -> p g j c", g=2, j=JT)
        o_nat = sb("o_nat", [P, ST, 256])
        alibi = sb("alibi", [P, NB])
        ident = sb("ident", [P, P])
        rows = sb("rows", [N_PAR, P])
        par = sb("par", [P, N_PAR])
        sp = sb("sp", [P, 10, 4])
        maxes = sb("maxes", [P, 2 * HEADS])
        sums = sb("sums", [P, 2, ST, 4])
        rsums = sb("rsums", [P, 2, ST, 4])
        row_sum = sb("row_sum", [P, ST, 2])
        mv = sb("mv", [P, ST, 4])
        centred = [t[:, :, :].rearrange("p j c -> p (j c)") for t in (qt, kt)]
        squares = vs[:, :, :].rearrange("p s c -> p (s c)")
        eps = sb("eps", [P, 1])

        bank = [ctx.enter_context(nc.psum_tensor(f"bank{n}", [P, BANK], F32)) for n in range(8)]

        x_in = [sem(f"x_in{n}") for n in range(2 * ST)]
        first_in = [sem(f"first_in{q}") for q in range(4 * FIRST)]
        first_hi, first_lo = sem("first_hi"), sem("first_lo")
        raw_in = [sem(f"raw_in{n}") for n in range(RING)]
        par_in, ln1_in, ln2_in, gw_in = sem("par_in"), sem("ln1_in"), sem("ln2_in"), sem("gw_in")
        out_done = sem("out_done")
        const_ok = sem("const_ok")
        pool_step = sem("pool_step")
        hi_ok, lo_ok = sem("hi_ok"), sem("lo_ok")
        par_t, par_ok, sp_z, sp_step, sp_ok = (sem("par_t"), sem("par_ok"), sem("sp_z"), sem("sp_step"),
                                               sem("sp_ok"))
        xt_t, xt_hi_ok, xt_lo_ok = sem("xt_t"), sem("xt_hi_ok"), sem("xt_lo_ok")
        proj_ok, proj_out = sem("proj_ok"), sem("proj_out")
        conv_step, conv_ok = sem("conv_step"), sem("conv_ok")
        gates_ok, gates_out = sem("gates_ok"), sem("gates_out")
        tanh_ok, decay_ok, decay2_ok = sem("tanh_ok"), sem("decay_ok"), sem("decay2_ok")
        root2_ok, root_ok, ix_ok, u_ok = sem("root2_ok"), sem("root_ok"), sem("ix_ok"), sem("u_ok")
        scan_ok, lru_ok, lru_hi, lru_lo = sem("scan_ok"), sem("lru_ok"), sem("lru_hi"), sem("lru_lo")
        score_ok, logit_ok, max_ok, prob_ok = sem("score_ok"), sem("logit_ok"), sem("max_ok"), sem("prob_ok")
        max_half = sem("max_half")
        pt_ok, pt_out, pv_ok = sem("pt_ok"), sem("pt_out"), sem("pv_ok")
        rsum_ok, norm_ok, ot_ok, ot_hi, ot_lo = (sem("rsum_ok"), sem("norm_ok"), sem("ot_ok"), sem("ot_hi"),
                                                 sem("ot_lo"))
        mix_ok, mix_part, res_ok, ln_step = sem("mix_ok"), sem("mix_part"), sem("res_ok"), sem("ln_step")
        mean_ok, var_ok, dev_ok, rdev_ok, x1_ok = sem("mean_ok"), sem("var_ok"), sem("dev_ok"), sem("rdev_ok"), sem("x1_ok")
        up_ok, relu_ok, sq_ok, hhi_ok, hlo_ok = (sem("up_ok"), sem("relu_ok"), sem("sq_ok"), sem("hhi_ok"),
                                                 sem("hlo_ok"))
        rows_ok, rows_out, turned = sem("rows_ok"), sem("rows_out"), sem("turned")
        down_ok, res2_ok, y_ok, out_ok = sem("down_ok"), sem("res2_ok"), sem("y_ok"), sem("out_ok")

        w_in_k = w_in[0].rearrange("(k p) c -> p k c", p=P)
        w_up_k = w_up[0].rearrange("(k p) c -> p k c", p=P)
        w_out_k = w_out[0].rearrange("(k p) c -> p k c", p=P)
        w_dn_k = w_down[0].rearrange("(k p) c -> p k c", p=P)

        def cols8(ring, slot):
            return ring[:, slot, :].rearrange("p (k c) -> p k c", k=8)

        def proj_bank(n):
            return n % 4 if n < 7 else (7 if n == 7 else (n - 8) % 3)

        def last_in(n):
            return max(m for m in range(n) if proj_bank(m) == proj_bank(n))

        def rows2(ring, slot):
            return ring[:, slot, :].rearrange("p (k c) -> p k c", k=2)

        block = ctx.enter_context(nc.Block())

        @block.sync
        def _(sp_e):
            def load_params():
                for c, v in ((C_CW, conv_w), (C_CB, conv_b), (C_BR, b_rg), (C_BI, b_ig), (C_LAM, lru_lambda),
                             (C_BUP, b_up)):
                    src = (v.rearrange("l t (j p) -> (l t j) p", p=P) if len(v.shape) == 3
                           else v.rearrange("l (j p) -> (l j) p", p=P))
                    sp_e.dma_start(rows[c:c + src.shape[0], :], src).then_inc(par_in, 16)

            def load_quarter(u, q):
                k = slice(2 * q, 2 * q + 2)
                sp_e.dma_start(cols8(w_raw, u)[:, k, :],
                               w_in_k[:, k, UNIT_COLS[u]:UNIT_COLS[u] + 256]).then_inc(first_in[4 * u + q], 16)

            for half in range(2):
                c = slice(half * HALF, (half + 1) * HALF)
                for s in range(ST):
                    sp_e.dma_start(xs[:, s, c], x[0, s * P:(s + 1) * P, c]).then_inc(x_in[2 * half + s], 16)
                for q in range(2 * half, 2 * half + 2):
                    load_quarter(0, q)
            for q in range(4):
                load_quarter(1, q)
            load_params()
            for u in range(2, FIRST):
                for q in range(4):
                    load_quarter(u, q)
            for n in range(FIRST, N_IN):
                c = UNIT_COLS[n]
                if n >= RING:
                    sp_e.wait_ge(lo_ok, n - RING + 1)
                sp_e.dma_start(cols8(w_raw, n % RING), w_in_k[:, :, c:c + 256]).then_inc(raw_in[n % RING], 16)
            for m, r in enumerate(OUT_ROWS):
                n = N_OUT0 + m
                sp_e.wait_ge(lo_ok, n - RING + 1)
                sp_e.dma_start(rows2(w_raw, n % RING),
                               w_out_k[:, r // P:r // P + 2, :]).then_inc(raw_in[n % RING], 16)

            def load_up(g, n):
                for m in range(2):
                    slot = (2 if isinstance(g, int) and g == 0 else 0) + m
                    sp_e.wait_ge(lo_ok, n + m - RING + 1)
                    sp_e.dma_start(cols8(w_raw, slot),
                                   w_up_k[:, :, bass.ds(g * 512 + m * 256, 256)]).then_inc(raw_in[slot], 16)

            def load_down(g, n, slot=2):
                for m in range(2):
                    sp_e.wait_ge(lo_ok, n + m - RING + 1)
                    sp_e.dma_start(rows2(w_raw, slot + m),
                                   w_dn_k[:, bass.ds(g * 4 + 2 * m, 2), :]).then_inc(raw_in[slot + m], 16)

            load_up(0, N_UP0)
            load_up(1, N_UP0 + 2)
            load_down(0, unit_d(0))
            with sp_e.Fori(1, GROUPS - 1) as g:
                load_up(g + 1, unit_u(g + 1))
                load_down(g, unit_d(g))
            load_down(GROUPS - 1, LAST_D, 0)
            for s in range(ST):
                for n in range(2):
                    sp_e.wait_ge(out_ok, 2 * s + n + 1)
                    sp_e.dma_start(out[0, s * P:(s + 1) * P, n * HALF:(n + 1) * HALF],
                                   xs[:, s, n * HALF:(n + 1) * HALF]).then_inc(out_done, 16)
            sp_e.wait_ge(out_done, 16 * 2 * ST)

        @block.gpsimd
        def _(pool):
            nc.gpsimd.memset(ident[:], 0.0).then_inc(pool_step, 1)
            pool.wait_ge(pool_step, 1)
            nc.gpsimd.affine_select(out=ident[:], in_=ident[:], compare_op=ALU.not_equal, fill=1.0, base=0,
                                    pattern=[[-1, P]], channel_multiplier=1).then_inc(const_ok, 1)
            nc.gpsimd.memset(xrp[:, :, 0:TAPS - 1], 0.0).then_inc(const_ok, 1)
            nc.gpsimd.memset(eps[:], LN_EPS).then_inc(const_ok, 1)
            nc.gpsimd.memset(gate_w, 0.0).then_inc(pool_step, 1)
            pool.wait_ge(pool_step, 2)
            pool.wait_ge(lo_ok, 1)
            for n, w in enumerate((w_rg, w_ig)):
                blocks = w[0].rearrange("(j h) e f -> h e j f", h=2)
                for h in range(2):
                    pool.dma_start(gate_w[h * BLK:(h + 1) * BLK, n, :, h * BLK:(h + 1) * BLK],
                                   blocks[h]).then_inc(gw_in, 16)
            nc.gpsimd.iota(alibi[:, 0:P], [[1, P]], base=0, channel_multiplier=-1,
                           allow_small_or_imprecise_dtypes=True).then_inc(pool_step, 1)
            nc.gpsimd.iota(alibi[:, P:NB], [[1, 2 * P]], base=-P, channel_multiplier=-1,
                           allow_small_or_imprecise_dtypes=True).then_inc(pool_step, 1)
            pool.wait_ge(pool_step, 4)
            nc.gpsimd.affine_select(out=alibi[:, 0:P], in_=alibi[:, 0:P], compare_op=ALU.is_ge, fill=NEG,
                                    base=0, pattern=[[-1, P]], channel_multiplier=1).then_inc(const_ok, 1)
            nc.gpsimd.affine_select(out=alibi[:, P:NB], in_=alibi[:, P:NB], compare_op=ALU.is_ge, fill=NEG,
                                    base=P, pattern=[[-1, 2 * P]], channel_multiplier=1).then_inc(const_ok, 1)
            pool.wait_ge(lo_ok, 5)
            for n, v in enumerate((ln1_g, ln1_b)):
                pool.dma_start(ln1[:, n, :], v[0:1, :].to_broadcast([P, D])).then_inc(ln1_in, 16)
            pool.wait_ge(lru_lo, 1)
            for dst, v in ((ln2[:, 0, :], ln2_g), (ln2[:, 1, :], ln2_b), (b_dn, b_down)):
                pool.dma_start(dst, v[0:1, :].to_broadcast([P, D])).then_inc(ln2_in, 16)

        @block.tensor
        def _(pe):
            def mm3(dst, a_hi, a_lo, b_hi, b_lo, start, stop):
                pe.matmul(dst, a_hi, b_hi, start=start, stop=False)
                pe.matmul(dst, a_hi, b_lo, start=False, stop=False)
                return pe.matmul(dst, a_lo, b_hi, start=False, stop=stop)

            def transpose_x(s, half, to):
                for q in range(4):
                    c = (4 * half + q) * P
                    t = pe.transpose(to[:, q * P:(q + 1) * P], xs[:, s, c:c + P], ident[:])
                t.then_inc(xt_t, 1)

            pe.wait_ge(const_ok, 1)

            def keep_busy(times):
                for n in range(times):
                    pe.transpose(bank[0][:, 0:P], ident[:], ident[:])

            keep_busy(WARM)

            def first_quarter(u, q):
                hi, lo = cols8(w_hi, u), cols8(w_lo, u)
                if u == 0:
                    pe.wait_ge(xt_lo_ok, 2 + 2 * (q // 2))
                if q < 3:
                    pe.wait_ge(first_lo, 3 * u + q + 1)
                else:
                    pe.wait_ge(lo_ok, u + 1)
                for n in range(2 * u, 2 * u + 2):
                    c = slice((n % 2) * P, (n % 2 + 1) * P)
                    for k in range(2 * q, 2 * q + 2):
                        i = mm3(bank[proj_bank(n)][:, 0:256], hi[:, k, c], lo[:, k, c], xt_hi[:, k, :], xt_lo[:, k, :],
                                k == 0, k == KT - 1)
                    if q == 3:
                        i.then_inc(proj_ok, 1)

            def proj(n):
                kind, j = TILES[n]
                u = n // 2
                slot = u % RING
                hi, lo = cols8(w_hi, slot), cols8(w_lo, slot)
                dst = bank[proj_bank(n)][:, 0:256]
                pe.wait_ge(lo_ok, u + 1)
                if n == 7:
                    pe.wait_ge(par_ok, 1)
                else:
                    pe.wait_ge(proj_out, last_in(n) + 1)
                for k in range(KT):
                    first, last = k == 0, k == KT - 1
                    if kind == "v":
                        s = slice((n % 2) * P, (n % 2 + 1) * P)
                        i = mm3(dst, xt_hi[:, k, s], xt_lo[:, k, s], hi[:, k, :], lo[:, k, :], first, last)
                    else:
                        c = slice((n % 2) * P, (n % 2 + 1) * P)
                        i = mm3(dst, hi[:, k, c], lo[:, k, c], xt_hi[:, k, :], xt_lo[:, k, :], first, last)
                i.then_inc(proj_ok, 1)

            def gates():
                pe.wait_ge(proj_out, 4)
                pe.wait_ge(gw_in, 4 * 16)
                for j in range(JT):
                    pe.wait_ge(conv_ok, j + 1)
                    for n in range(2):
                        i = pe.matmul(bank[3 + j][:, n * SEQ:(n + 1) * SEQ], gate_w[:, n, j, :],
                                      xc[:, j * SEQ:(j + 1) * SEQ], start=True, stop=True)
                    i.then_inc(gates_ok, 1)

            def scores(h):
                b, j, r = bank[4 + h % 2], h // 2, slice(DH * (h % 2), DH * (h % 2) + DH)
                if h == 0:
                    pe.wait_ge(gates_out, 2 * JT)
                pe.wait_ge(proj_out, (15, 16, 19, 20)[j])
                if h >= 2:
                    pe.wait_ge(logit_ok, h - 1)
                pe.matmul(b[:, 0:P], qt[r, j, 0:P], kt[r, j, 0:P], start=True, stop=True)
                pe.matmul(b[:, P:NB], qt[r, j, P:SEQ], kt[r, j, :], start=True, stop=True).then_inc(score_ok, 1)

            def turn_prob(h):
                pe.wait_ge(prob_ok, 2 * (h + 1))
                if h >= 1:
                    pe.wait_ge(pt_out, h)
                for q in range(3):
                    t = pe.transpose(bank[7][:, q * P:(q + 1) * P], prob[:, h % 2, q * P:(q + 1) * P], ident[:])
                t.then_inc(pt_ok, 1)

            def values(h):
                pe.wait_ge(pt_out, h + 1)
                if h == 4:
                    pe.wait_ge(norm_ok, 1)
                v = slice(h * DH, (h + 1) * DH)
                c = (h % 4) * DH
                pt = prob_t[:, h % 2, :]
                pe.matmul(bank[6][:, c:c + DH], pt[:, 0:P], vs[:, 0, v], start=True, stop=True)
                pe.matmul(bank[6][:, 256 + c:256 + c + DH], pt[:, P:2 * P], vs[:, 0, v], start=True, stop=False)
                pe.matmul(bank[6][:, 256 + c:256 + c + DH], pt[:, 2 * P:NB], vs[:, 1, v],
                          start=False, stop=True).then_inc(pv_ok, 1)

            def turn_out(part):
                b = bank[3] if part == 0 else bank[7]
                pe.wait_ge(norm_ok, part + 1)
                if part == 1:
                    pe.wait_ge(pt_out, HEADS)
                for k in range(2):
                    for s in range(ST):
                        t = pe.transpose(b[:, k * SEQ + s * P:k * SEQ + (s + 1) * P],
                                         o_nat[:, s, k * P:(k + 1) * P], ident[:])
                t.then_inc(ot_ok, 1)

            def mix(s, n, part):
                units = {0: (10, 11), 1: (12,), 2: (13,)}[part]
                rows_at = {0: 4, 1: 0, 2: 2}[part]
                if part == 0:
                    pe.wait_ge(lru_lo, 1)
                    pe.wait_ge(proj_out, 20)
                    if s == 1 and n == 1:
                        pe.wait_ge(ot_lo, 1)
                else:
                    pe.wait_ge(ot_lo, part)
                for a, u in enumerate(units):
                    pe.wait_ge(lo_ok, u + 1)
                    for b in range(2):
                        k = rows_at + 2 * a + b
                        c = slice(n * HALF, (n + 1) * HALF)
                        i = mm3(bank[2 * s + n][:, :], cat_hi[:, k, s * P:(s + 1) * P],
                                cat_lo[:, k, s * P:(s + 1) * P], rows2(w_hi, u % RING)[:, b, c],
                                rows2(w_lo, u % RING)[:, b, c], k == 4, k == 3)
                if part == 2:
                    i.then_inc(mix_ok, 1)
                elif s == 1 and n == 1:
                    i.then_inc(mix_part, 1)

            for half in range(2):
                for s in range(ST):
                    pe.wait_ge(x_in[2 * half + s], 16)
                    transpose_x(s, half, bank[4 + 2 * half + s])
                if half == 0:
                    keep_busy(WARM_MORE)
            for q in range(4):
                first_quarter(0, q)
            for q in range(4):
                if q == 3:
                    pe.wait_ge(par_in, 6 * 16)
                    pe.transpose(bank[7][:, 0:N_PAR], rows[:, :], ident[0:N_PAR, 0:N_PAR]).then_inc(par_t, 1)
                first_quarter(1, q)
            for n in range(4, 8):
                proj(n)
            gates()
            for n in range(8, 16):
                proj(n)
            pe.wait_ge(const_ok, 5)
            scores(0)
            scores(1)
            proj(16)
            turn_prob(0)
            scores(2)
            proj(17)
            values(0)
            turn_prob(1)
            scores(3)
            proj(18)
            values(1)
            turn_prob(2)
            proj(19)
            values(2)
            turn_prob(3)
            scores(4)
            scores(5)
            values(3)
            mix(0, 0, 0)
            turn_prob(4)
            scores(6)
            turn_prob(5)
            values(4)
            turn_out(0)
            scores(7)
            mix(0, 1, 0)
            turn_prob(6)
            values(5)
            turn_prob(7)
            values(6)
            mix(0, 0, 1)
            values(7)
            mix(0, 1, 1)
            turn_out(1)
            mix(1, 0, 0)
            mix(0, 0, 2)
            mix(0, 1, 2)
            mix(1, 1, 0)
            mix(1, 0, 1)
            mix(1, 1, 1)
            for half in range(2):
                pe.wait_ge(x1_ok, half + 1)
                transpose_x(0, half, bank[6 + half])
            mix(1, 0, 2)
            mix(1, 1, 2)

            def up(g, n, par2):
                for m in range(2):
                    hi, lo = cols8(w_hi, m), cols8(w_lo, m)
                    pe.wait_ge(lo_ok, n + m + 1)
                    pe.wait_ge(relu_ok, 4 * g - 6 + 2 * m)
                    for f in range(2):
                        for k in range(KT):
                            i = mm3(bank[4 + 2 * par2 + m][:, f * SEQ:(f + 1) * SEQ], hi[:, k, f * P:(f + 1) * P],
                                    lo[:, k, f * P:(f + 1) * P], xt_hi[:, k, :], xt_lo[:, k, :],
                                    k == 0, k == KT - 1)
                    i.then_inc(up_ok, 1)

            def up_rows(g, s, at=None, between=None):
                base, n0 = (2, N_UP0) if g == 0 else (0, N_UP0 + 2)
                for m in range(2):
                    hi, lo = (u14_hi, u14_lo) if n0 + m == N_UP0 else (cols8(w_hi, base + m), cols8(w_lo, base + m))
                    pe.wait_ge(lo_ok, n0 + m + 1)
                    for k in range(KT):
                        if m == 0 and k % 4 == 0:
                            pe.wait_ge(xt_lo_ok, 4 + 2 * s + k // 4 + 1)
                        if at == (m, k):
                            between()
                        i = mm3(bank[2 * s + g][:, m * 256:(m + 1) * 256], xt_hi[:, k, s * P:(s + 1) * P],
                                xt_lo[:, k, s * P:(s + 1) * P], hi[:, k, :], lo[:, k, :], k == 0, k == KT - 1)
                    i.then_inc(rows_ok, 1)

            def turn_rows(nth, g, s):
                pe.wait_ge(rows_out, nth + 1)
                for f in range(FG):
                    b = bank[4 + 2 * g + f // 2]
                    a = (f % 2) * SEQ + s * P
                    i = pe.transpose(b[:, a:a + P], h_rows[:, nth % 2, f * P:(f + 1) * P], ident[:])
                    if s == 1 and f % 2 == 1:
                        i.then_inc(up_ok, 1)
                    elif f == FG - 1:
                        i.then_inc(turned, 1)

            def down_first():
                for m in range(2):
                    pe.wait_ge(hlo_ok, m + 1)
                    pe.wait_ge(lo_ok, unit_d(0) + m + 1)
                    for s in range(ST):
                        for n in range(2):
                            if m == 0 and s == 0 and n == 1:
                                turn_rows(3, 1, 1)
                            for f in range(2 * m, 2 * m + 2):
                                i = mm3(bank[2 * s + n][:, :], ht_hi[:, 0, f, s * P:(s + 1) * P],
                                        ht_lo[:, 0, f, s * P:(s + 1) * P],
                                        rows2(w_hi, 2 + m)[:, f % 2, n * HALF:(n + 1) * HALF],
                                        rows2(w_lo, 2 + m)[:, f % 2, n * HALF:(n + 1) * HALF], f == 0, False)
                i.then_inc(down_ok, 1)

            def down(g, par2, last=False):
                slot = 0 if last else 2
                pe.wait_ge(hlo_ok, 2 * g + 2)
                for s in range(ST):
                    for n in range(2):
                        c = slice(n * HALF, (n + 1) * HALF)
                        for f in range(FG):
                            if s == 0 and n == 0 and f % 2 == 0:
                                pe.wait_ge(lo_ok, (LAST_D if last else unit_d(g)) + f // 2 + 1)
                            i = mm3(bank[2 * s + n][:, :], ht_hi[:, par2, f, s * P:(s + 1) * P],
                                    ht_lo[:, par2, f, s * P:(s + 1) * P], rows2(w_hi, slot + f // 2)[:, f % 2, c],
                                    rows2(w_lo, slot + f // 2)[:, f % 2, c], False, last and f == FG - 1)
                        if last:
                            i.then_inc(y_ok, 1)
                if not last:
                    i.then_inc(down_ok, 1)

            up_rows(0, 0)

            def turn_x1():
                for half in range(2):
                    pe.wait_ge(x1_ok, 2 + half + 1)
                    transpose_x(1, half, bank[2 + half])

            up_rows(1, 0, (1, 6), turn_x1)
            turn_rows(0, 0, 0)
            up_rows(0, 1, (0, 4), lambda: turn_rows(1, 1, 0))
            up_rows(1, 1, (0, 4), lambda: turn_rows(2, 0, 1))
            pe.wait_ge(rows_out, 3)
            down_first()
            with pe.Fori(1, GROUPS - 1, 2) as g:
                for q in range(2):
                    up(g + q + 1, unit_u(g + q + 1), q)
                    down(g + q, 1 - q)
            down(GROUPS - 1, 1, last=True)

        @block.scalar
        def _(act):
            A = nc.scalar.activation
            def x_hi(n, s, half, src):
                act.wait_ge(xt_t, n + 1)
                nc.scalar.copy(xt_hi[:, 4 * half:4 * half + 4, s * P:(s + 1) * P],
                               src[:, :].rearrange("p (k c) -> p k c", k=4)).then_inc(xt_hi_ok, 1)

            def unit_hi(slot, nth, user, uses):
                if slot < FIRST:
                    nth = nth - 1
                act.wait_ge(raw_in[slot], 16 * nth)
                if user is not None:
                    act.wait_ge(user, uses)
                nc.scalar.copy(w_hi[:, slot, :], w_raw[:, slot, :]).then_inc(hi_ok, 1)

            def first_hi_part(u, q):
                k = slice(2 * q, 2 * q + 2)
                act.wait_ge(first_in[4 * u + q], 16)
                nc.scalar.copy(cols8(w_hi, u)[:, k, :], cols8(w_raw, u)[:, k, :]).then_inc(
                    first_hi if q < 3 else hi_ok, 1)

            def u_hi(n):
                if n < RING:
                    user, uses = None, 0
                elif n < RING + N_IN:
                    user, uses = proj_ok, 2 * (n - RING + 1)
                else:
                    user, uses = ((mix_part, 1), (mix_part, 2), (mix_ok, 4))[n - N_UP0 - 1]
                unit_hi(n % RING, n // RING + 1, user, uses)

            def proj_evict(n):
                kind, j = TILES[n]
                src = bank[proj_bank(n)][:, 0:256]
                act.wait_ge(proj_ok, n + 1)
                if kind == "xr":
                    i = nc.scalar.copy(xrp[:, j, TAPS - 1:], src)
                elif kind == "gr":
                    i = A(gelu[:, j * SEQ:(j + 1) * SEQ], src, ACT.Gelu_apprx_tanh)
                elif kind == "v":
                    i = nc.scalar.copy(vs[:, j % 2, (j // 2) * 256:(j // 2 + 1) * 256], src)
                elif kind == "k":
                    i = nc.scalar.copy(kt[:, j, :], src)
                else:
                    i = nc.scalar.mul(qt[:, j, :], src, SCALE)
                i.then_inc(proj_out, 1)

            def exps(h):
                act.wait_ge(max_ok, h + 1)
                for s, c in ((0, slice(0, P)), (1, slice(P, NB))):
                    A(prob[:, h % 2, c], prob[:, h % 2, c], ACT.Exp, bias=maxes[:, 2 * h + s:2 * h + s + 1],
                      accum_out=sums[:, h // 4, s, h % 4:h % 4 + 1]).then_inc(prob_ok, 1)

            def out_hi(part):
                b = bank[3] if part == 0 else bank[7]
                act.wait_ge(ot_ok, part + 1)
                nc.scalar.copy(cat_hi[:, 2 * part:2 * part + 2, :],
                               b[:, :].rearrange("p (k c) -> p k c", k=2)).then_inc(ot_hi, 1)

            for half in range(2):
                for s in range(ST):
                    x_hi(2 * half + s, s, half, bank[4 + 2 * half + s])
                first_hi_part(0, 2 * half)
                first_hi_part(0, 2 * half + 1)
            for q in range(4):
                first_hi_part(1, q)
            for q in range(4):
                first_hi_part(2, q)
            act.wait_ge(const_ok, 2)
            proj_evict(0)
            proj_evict(1)
            u_hi(3)
            u_hi(4)
            act.wait_ge(sp_step, 2)
            A(sp[:, 1, :], sp[:, 0, :], ACT.Exp, scale=-1.0).then_inc(sp_z, 1)
            for n in range(2, 8):
                proj_evict(n)
                if n % 2:
                    u_hi(n // 2 + 4)
            for j in range(JT):
                act.wait_ge(gates_ok, j + 1)
                for n, (dst, c) in enumerate(((gate_r, C_BR), (gate_i, C_BI))):
                    A(dst[:, j * SEQ:(j + 1) * SEQ], bank[3 + j][:, n * SEQ:(n + 1) * SEQ], ACT.Sigmoid,
                      bias=par[:, c + j:c + j + 1]).then_inc(gates_out, 1)
            proj_evict(8)
            proj_evict(9)
            u_hi(8)
            act.wait_ge(sp_ok, 2)
            act.wait_ge(gates_out, 2 * JT)
            act.wait_ge(conv_ok, JT)
            for j in range(JT):
                c = slice(j * SEQ, (j + 1) * SEQ)
                A(root[:, c], gate_r[:, c], ACT.Tanh, scale=sp[:, 8, j:j + 1]).then_inc(tanh_ok, 1)
            for j in range(JT):
                c = slice(j * SEQ, (j + 1) * SEQ)
                A(decay[:, c], gate_r[:, c], ACT.Exp, scale=sp[:, 9, j:j + 1]).then_inc(decay_ok, 1)
            proj_evict(10)
            act.wait_ge(decay_ok, JT)
            act.wait_ge(tanh_ok, JT)
            A(gate_r, decay, ACT.Square).then_inc(decay2_ok, 1)
            proj_evict(11)
            u_hi(9)
            act.wait_ge(root2_ok, 1)
            A(root, root, ACT.Sqrt).then_inc(root_ok, 1)
            proj_evict(12)
            proj_evict(13)
            proj_evict(14)
            proj_evict(15)
            exps(0)
            exps(1)
            act.wait_ge(lru_ok, 1)
            nc.scalar.copy(cat_hi[:, 4:8, :], gelu.rearrange("p (k c) -> p k c", k=4)).then_inc(lru_hi, 1)
            proj_evict(16)
            u_hi(10)
            exps(2)
            proj_evict(17)
            u_hi(11)
            exps(3)
            proj_evict(18)
            u_hi(12)
            proj_evict(19)
            u_hi(13)
            exps(4)
            exps(5)
            out_hi(0)
            exps(6)
            exps(7)
            act.wait_ge(raw_in[2], 16 * 3)
            nc.scalar.copy(u14_hi, cols8(w_raw, 2)).then_inc(hi_ok, 1)
            out_hi(1)

            def deviation(i, s):
                act.wait_ge(mean_ok, i + 1)
                A(squares, xs[:, s, :], ACT.Square, bias=mv[:, s, 0:1], accum_out=mv[:, s, 1:2]).then_inc(var_ok, 1)
                act.wait_ge(var_ok, i + 1)
                A(mv[:, s, 2:3], mv[:, s, 1:2], ACT.Sqrt, bias=eps[:], scale=1.0 / D).then_inc(dev_ok, 1)

            deviation(0, 0)
            u_hi(15)
            x_hi(4, 0, 0, bank[6])
            x_hi(5, 0, 1, bank[7])
            u_hi(16)
            u_hi(17)
            act.wait_ge(ln2_in, 3 * 16)

            def rows_evict(nth, g, s):
                act.wait_ge(rows_ok, 2 * nth + 2)
                if nth == 2:
                    act.wait_ge(turned, 1)
                elif nth == 3:
                    act.wait_ge(turned, 2)
                nc.scalar.copy(h_rows[:, nth % 2, :], bank[2 * s + g][:, :]).then_inc(rows_out, 1)

            rows_evict(0, 0, 0)
            deviation(1, 1)
            x_hi(6, 1, 0, bank[2])
            x_hi(7, 1, 1, bank[3])
            rows_evict(1, 1, 0)
            unit_hi(2, 5, mix_part, 1)
            rows_evict(2, 0, 1)

            def hidden(g, par2, m):
                pe_pair = 2 * g + m
                act.wait_ge(up_ok, pe_pair + 1)
                if not (isinstance(g, int) and g == 0):
                    act.wait_ge(hlo_ok, pe_pair - 1)
                for f in range(2):
                    A(relu_h[:, m, f * SEQ:(f + 1) * SEQ], bank[4 + 2 * par2 + m][:, f * SEQ:(f + 1) * SEQ],
                      ACT.Relu, bias=par[:, bass.ds(C_BUP + 4 * g + 2 * m + f, 1)]).then_inc(relu_ok, 1)
                act.wait_ge(relu_ok, 2 * pe_pair + 2)
                A(ht_hi[:, par2, 2 * m:2 * m + 2, :], relu_h[:, m, :].rearrange("p (k c) -> p k c", k=2),
                  ACT.Square).then_inc(hhi_ok, 1)

            def down_hi(g):
                for m in range(2):
                    unit_hi(2 + m, g + 5, down_ok, g)

            hidden(0, 0, 0)
            hidden(0, 0, 1)
            unit_hi(3, 5, rows_ok, 6)
            rows_evict(3, 1, 1)
            with act.Fori(1, GROUPS - 1, 2) as g:
                for q in range(2):
                    for m in range(2):
                        hidden(g + q, 1 - q, m)
                        unit_hi(m, g + q + 5, up_ok, 2 * (g + q) + m + 1)
                    down_hi(g + q)
            hidden(GROUPS - 1, 1, 0)
            hidden(GROUPS - 1, 1, 1)
            for m in range(2):
                unit_hi(m, GROUPS + 4, up_ok, 2 * (GROUPS - 1) + m + 1)
            deviation(2, 0)
            deviation(3, 1)

        @block.vector
        def _(dve):
            V = nc.vector

            def x_lo(n, s, half, src):
                dst = (slice(None), slice(4 * half, 4 * half + 4), slice(s * P, (s + 1) * P))
                dve.wait_ge(xt_hi_ok, n + 1)
                V.tensor_tensor(xt_lo[dst], src[:, :].rearrange("p (k c) -> p k c", k=4),
                                xt_hi[dst].bitcast(F32), ALU.subtract).then_inc(xt_lo_ok, 1)

            def unit_lo(n, slot):
                dve.wait_ge(hi_ok, n + 1)
                V.tensor_tensor(w_lo[:, slot, :], w_raw[:, slot, :], w_hi[:, slot, :].bitcast(F32),
                                ALU.subtract).then_inc(lo_ok, 1)

            def u_lo(n):
                unit_lo(n, n % RING)

            sp_steps = [0]

            def step(i):
                sp_steps[0] += 1
                i.then_inc(sp_step, 1)
                dve.wait_ge(sp_step, sp_steps[0])

            def first_lo_part(u, q):
                k = slice(2 * q, 2 * q + 2)
                if q < 3:
                    dve.wait_ge(first_hi, 3 * u + q + 1)
                else:
                    dve.wait_ge(hi_ok, u + 1)
                V.tensor_tensor(cols8(w_lo, u)[:, k, :], cols8(w_raw, u)[:, k, :],
                                cols8(w_hi, u)[:, k, :].bitcast(F32), ALU.subtract).then_inc(
                    first_lo if q < 3 else lo_ok, 1)

            for half in range(2):
                for s in range(ST):
                    x_lo(2 * half + s, s, half, bank[4 + 2 * half + s])
                first_lo_part(0, 2 * half)
                first_lo_part(0, 2 * half + 1)
            for q in range(4):
                first_lo_part(1, q)
            for q in range(4):
                first_lo_part(2, q)
            dve.wait_ge(par_t, 1)
            V.tensor_copy(par[:], bank[7][:, 0:N_PAR]).then_inc(par_ok, 1)
            dve.wait_ge(par_ok, 1)
            lam = par[:, C_LAM:C_LAM + 4]
            step(V.tensor_scalar(sp[:, 2, :], lam, -1.0, None, ALU.mult))
            step(V.tensor_tensor(sp[:, 0, :], lam, sp[:, 2, :], ALU.max))

            def conv(j):
                dst = xc[:, j * SEQ:(j + 1) * SEQ]
                dve.wait_ge(proj_out, j + 1)
                V.tensor_scalar(dst, xrp[:, j, 0:SEQ], par[:, C_CW + j:C_CW + j + 1],
                                par[:, C_CB + j:C_CB + j + 1], ALU.mult, ALU.add).then_inc(conv_step, 1)
                for t in range(1, TAPS):
                    dve.wait_ge(conv_step, 3 * j + t)
                    c = C_CW + JT * t + j
                    V.scalar_tensor_tensor(dst, xrp[:, j, t:t + SEQ], par[:, c:c + 1], dst, ALU.mult,
                                           ALU.add).then_inc(conv_ok if t == TAPS - 1 else conv_step, 1)

            dve.wait_ge(const_ok, 2)
            conv(0)
            u_lo(3)
            conv(1)
            u_lo(4)
            conv(2)
            conv(3)
            u_lo(5)
            u_lo(6)
            u_lo(7)

            dve.wait_ge(sp_z, 1)
            step(V.tensor_scalar(sp[:, 3, :], sp[:, 1, :], 2.0, None, ALU.add))
            step(V.reciprocal(sp[:, 4, :], sp[:, 3, :]))
            step(V.tensor_tensor(sp[:, 5, :], sp[:, 1, :], sp[:, 4, :], ALU.mult))
            step(V.tensor_tensor(sp[:, 6, :], sp[:, 5, :], sp[:, 5, :], ALU.mult))
            step(V.tensor_scalar(sp[:, 7, :], sp[:, 6, :], 1.0 / 15, None, ALU.mult))
            for c in (13, 11, 9, 7, 5, 3):
                step(V.scalar_tensor_tensor(sp[:, 7, :], sp[:, 7, :], 1.0 / c, sp[:, 6, :], ALU.add, ALU.mult))
            step(V.scalar_tensor_tensor(sp[:, 7, :], sp[:, 7, :], 1.0, sp[:, 5, :], ALU.add, ALU.mult))
            step(V.tensor_scalar(sp[:, 2, :], sp[:, 2, :], 0.0, 8.0, ALU.max, ALU.mult))
            V.scalar_tensor_tensor(sp[:, 8, :], sp[:, 7, :], 16.0, sp[:, 2, :], ALU.mult, ALU.add).then_inc(sp_ok, 1)
            dve.wait_ge(sp_ok, 1)
            V.tensor_scalar(sp[:, 9, :], sp[:, 8, :], -1.0, None, ALU.mult).then_inc(sp_ok, 1)

            dve.wait_ge(gates_out, 2 * JT)
            V.tensor_tensor(gate_i, gate_i, xc, ALU.mult).then_inc(ix_ok, 1)
            u_lo(8)
            dve.wait_ge(decay2_ok, 1)
            V.scalar_tensor_tensor(root, gate_r, 1.0, root, ALU.add, ALU.mult).then_inc(u_ok, 1)
            dve.wait_ge(u_ok, 1)
            V.tensor_scalar(root, root, 1e-34, None, ALU.max).then_inc(root2_ok, 1)
            u_lo(9)
            dve.wait_ge(root_ok, 1)
            dve.wait_ge(ix_ok, 1)
            V.tensor_tensor(gate_i, gate_i, root, ALU.mult).then_inc(u_ok, 1)
            dve.wait_ge(u_ok, 2)
            for j in range(JT):
                c = slice(j * SEQ, (j + 1) * SEQ)
                V.tensor_tensor_scan(xc[:, c], decay[:, c], gate_i[:, c], 0.0, ALU.mult, ALU.add).then_inc(scan_ok, 1)
            dve.wait_ge(scan_ok, JT)
            V.tensor_tensor(gelu, gelu, xc, ALU.mult).then_inc(lru_ok, 1)
            def lru_split():
                dve.wait_ge(lru_hi, 1)
                V.tensor_tensor(cat_lo[:, 4:8, :], gelu.rearrange("p (k c) -> p k c", k=4),
                                cat_hi[:, 4:8, :].bitcast(F32), ALU.subtract).then_inc(lru_lo, 1)

            def logits(h):
                dve.wait_ge(score_ok, h + 1)
                if h >= 2:
                    dve.wait_ge(pt_ok, h - 1)
                V.scalar_tensor_tensor(prob[:, h % 2, :], alibi[:], SLOPES[h], bank[4 + h % 2][:, 0:NB],
                                       ALU.mult, ALU.add).then_inc(logit_ok, 1)
                dve.wait_ge(logit_ok, h + 1)
                m = maxes[:, 2 * h:2 * h + 2]
                V.tensor_reduce(m[:, 0:1], prob[:, h % 2, 0:P], AX.X, ALU.max, negate=True).then_inc(max_half, 1)
                V.tensor_reduce(m[:, 1:2], prob[:, h % 2, P:NB], AX.X, ALU.max, negate=True).then_inc(max_ok, 1)

            def prob_out(h):
                dve.wait_ge(pt_ok, h + 1)
                if h >= 2:
                    dve.wait_ge(pv_ok, h - 1)
                V.tensor_copy(prob_t[:, h % 2, :], bank[7][:, 0:NB]).then_inc(pt_out, 1)

            def normalise(part):
                dve.wait_ge(prob_ok, 8 * (part + 1))
                V.reciprocal(rsums[:, part, :, :], sums[:, part, :, :]).then_inc(rsum_ok, 1)
                dve.wait_ge(rsum_ok, part + 1)
                dve.wait_ge(pv_ok, 4 * (part + 1))
                if part == 1:
                    dve.wait_ge(ot_ok, 1)
                V.tensor_tensor(o_nat[:, :, :].rearrange("p s (h d) -> p (s h) d", h=4),
                                bank[6][:, :].rearrange("p (a d) -> p a d", d=DH),
                                rsums[:, part, :, :].rearrange("p s h -> p (s h)").unsqueeze(2).to_broadcast([P, 2 * 4, DH]),
                                ALU.mult).then_inc(norm_ok, 1)

            def out_lo(part):
                b = bank[3] if part == 0 else bank[7]
                dve.wait_ge(ot_hi, part + 1)
                V.tensor_tensor(cat_lo[:, 2 * part:2 * part + 2, :], b[:, :].rearrange("p (k c) -> p k c", k=2),
                                cat_hi[:, 2 * part:2 * part + 2, :].bitcast(F32), ALU.subtract).then_inc(ot_lo, 1)

            dve.wait_ge(const_ok, 5)
            logits(0)
            logits(1)
            prob_out(0)
            lru_split()
            logits(2)
            u_lo(10)
            prob_out(1)
            logits(3)
            u_lo(11)
            prob_out(2)
            u_lo(12)
            prob_out(3)
            logits(4)
            logits(5)
            normalise(0)
            prob_out(4)
            logits(6)
            prob_out(5)
            logits(7)
            out_lo(0)
            prob_out(6)
            prob_out(7)
            u_lo(13)
            normalise(1)
            dve.wait_ge(hi_ok, N_UP0 + 1)
            V.tensor_tensor(u14_lo, cols8(w_raw, 2), u14_hi.bitcast(F32), ALU.subtract).then_inc(lo_ok, 1)
            out_lo(1)

            def layer_norm(i, s, gain, shift, residual, done):
                for n in range(2):
                    residual(n)
                dve.wait_ge(res_ok, 2 * i + 2)
                V.tensor_scalar(mv[:, s, 0:1], row_sum[:, s, 0:1], row_sum[:, s, 1:2], -1.0 / D, ALU.add,
                                ALU.mult).then_inc(mean_ok, 1)
                dve.wait_ge(mean_ok, i + 1)
                for n in range(2):
                    c = slice(n * HALF, (n + 1) * HALF)
                    V.scalar_tensor_tensor(centred[s][:, c], xs[:, s, c], mv[:, s, 0:1], gain[:, c], ALU.add,
                                           ALU.mult).then_inc(ln_step, 1)
                dve.wait_ge(dev_ok, i + 1)
                V.reciprocal(mv[:, s, 3:4], mv[:, s, 2:3]).then_inc(rdev_ok, 1)
                dve.wait_ge(rdev_ok, i + 1)
                for n in range(2):
                    c = slice(n * HALF, (n + 1) * HALF)
                    dve.wait_ge(ln_step, 2 * i + n + 1)
                    V.scalar_tensor_tensor(xs[:, s, c], centred[s][:, c], mv[:, s, 3:4], shift[:, c], ALU.mult,
                                           ALU.add).then_inc(done, 1)

            def ln1_of(s):
                def residual(n):
                    c = slice(n * HALF, (n + 1) * HALF)
                    dve.wait_ge(mix_ok, 2 * s + n + 1)
                    V.scalar_tensor_tensor(xs[:, s, c], xs[:, s, c], ALPHA, bank[2 * s + n][:, :], ALU.mult,
                                           ALU.add, accum_out=row_sum[:, s, n:n + 1]).then_inc(res_ok, 1)
                layer_norm(s, s, ln1[:, 0, :], ln1[:, 1, :], residual, x1_ok)

            dve.wait_ge(ln1_in, 2 * 16)
            ln1_of(0)
            x_lo(4, 0, 0, bank[6])
            x_lo(5, 0, 1, bank[7])
            u_lo(15)
            u_lo(16)
            u_lo(17)
            ln1_of(1)
            x_lo(6, 1, 0, bank[2])
            x_lo(7, 1, 1, bank[3])
            unit_lo(unit_d(0), 2)
            dve.wait_ge(ln2_in, 3 * 16)
            for s in range(ST):
                V.scalar_tensor_tensor(xs[:, s, :], xs[:, s, :], ALPHA, b_dn, ALU.mult, ALU.add).then_inc(res2_ok, 1)

            def hidden(g, par2, m):
                pair = 2 * g + m
                dve.wait_ge(relu_ok, 2 * pair + 2)
                V.tensor_tensor(sq_h[:, m, :], relu_h[:, m, :], relu_h[:, m, :], ALU.mult).then_inc(sq_ok, 1)
                dve.wait_ge(sq_ok, pair + 1)
                dve.wait_ge(hhi_ok, pair + 1)
                V.tensor_tensor(ht_lo[:, par2, 2 * m:2 * m + 2, :], sq_h[:, m, :].rearrange("p (k c) -> p k c", k=2),
                                ht_hi[:, par2, 2 * m:2 * m + 2, :].bitcast(F32), ALU.subtract).then_inc(hlo_ok, 1)

            def down_lo(g):
                for m in range(2):
                    unit_lo(unit_d(g) + m, 2 + m)

            hidden(0, 0, 0)
            hidden(0, 0, 1)
            unit_lo(unit_d(0) + 1, 3)
            with dve.Fori(1, GROUPS - 1, 2) as g:
                for q in range(2):
                    for m in range(2):
                        hidden(g + q, 1 - q, m)
                        unit_lo(unit_u(g + q + 1) + m, m)
                    down_lo(g + q)
            hidden(GROUPS - 1, 1, 0)
            hidden(GROUPS - 1, 1, 1)
            for m in range(2):
                unit_lo(LAST_D + m, m)

            dve.wait_ge(res2_ok, ST)
            for s in range(ST):
                def residual(n, s=s):
                    c = slice(n * HALF, (n + 1) * HALF)
                    dve.wait_ge(y_ok, 2 * s + n + 1)
                    V.scalar_tensor_tensor(xs[:, s, c], xs[:, s, c], 1.0, bank[2 * s + n][:, :], ALU.mult, ALU.add,
                                           accum_out=row_sum[:, s, n:n + 1]).then_inc(res_ok, 1)
                layer_norm(2 + s, s, ln2[:, 0, :], ln2[:, 1, :], residual, out_ok)


_INS = ["x", "w_in", "conv_w", "conv_b", "w_rg", "b_rg", "w_ig", "b_ig", "lru_lambda", "w_out",
        "ln1_g", "ln1_b", "w_up", "b_up", "w_down", "b_down", "ln2_g", "ln2_b"]


def kernel(**inputs):
    import numpy as _np
    import concourse.bacc as _bacc
    from concourse import mybir as _mybir
    from concourse.bass_utils import run_bass_kernel_spmd as _run

    nc = _bacc.Bacc("TRN2", target_bir_lowering=False, num_devices=1)
    arrays, args = {}, []
    for name in _INS:
        a = _np.ascontiguousarray(inputs[name])
        arrays[f"in_{name}_dram"] = a
        args.append(nc.dram_tensor(f"in_{name}_dram", a.shape, _mybir.dt.from_np(a.dtype), kind="ExternalInput").ap())
    out = nc.dram_tensor("out_dram", inputs["x"].shape, _mybir.dt.float32, kind="ExternalOutput").ap()
    hybrid_layer(nc, *args, out)
    r = _run(nc, [arrays], core_ids=[0])
    return r.results[0]["out_dram"]
```
